# Optimizing a Trainium2 kernel written in Bass

```python
import math
import jax
import jax.numpy as jnp
from jax import lax
import numpy as np
import jax, jax.numpy as jnp

D_MODEL = 1024
BATCH = 1
SEQ = 256
DEPTH = 2

GRID_W = 64
CTX_LEN = 256
MIX_WIDTH = D_MODEL
A_WIDTH = MIX_WIDTH // 2
B_WIDTH = MIX_WIDTH - A_WIDTH
SHORT_CONV_W = 3
CONFORMER_CONV_W = 31
AB_IN = 3 * A_WIDTH + 2 * B_WIDTH
C_HEAD_DIM = 64
C_V_DIM = 2 * C_HEAD_DIM
C_HEADS = (MIX_WIDTH // 2) // C_V_DIM
C_QK = C_HEADS * 2 * C_HEAD_DIM
C_V = C_HEADS * C_V_DIM
HY_WIDTH = MIX_WIDTH - C_V
CD_IN = 2 * C_QK + C_V + 3 * HY_WIDTH
Q_BLOCK = 128
ROPE_THETA = 10000.0
HY_BANDS = 16
HY_EMB = 2 * HY_BANDS + 1
HY_ORDER = 64
HY_MIN_DECAY = math.log(1e-2) / 1.5
HY_MAX_DECAY = math.log(1e-2) / 0.3
N_EXPERTS = 16
EXPERT_FF = 1024
EC_CAPACITY = 2
NORM_EPS = 1e-6
SUBLN_EPS = 1e-5


def rms_norm(x, g, eps=NORM_EPS):
    xf = x.astype(jnp.float32)
    y = xf * lax.rsqrt(jnp.mean(jnp.square(xf), axis=-1, keepdims=True) + eps)
    return (y * g.astype(jnp.float32)).astype(x.dtype)

def layer_norm(x, g, b, eps=NORM_EPS):
    xf = x.astype(jnp.float32)
    mu = jnp.mean(xf, axis=-1, keepdims=True)
    var = jnp.mean(jnp.square(xf - mu), axis=-1, keepdims=True)
    y = (xf - mu) * lax.rsqrt(var + eps)
    return (y * g.astype(jnp.float32) + b.astype(jnp.float32)).astype(x.dtype)

def modulate(h, shift, scale):
    return h * (1 + scale) + shift

def depthwise_conv(u, w):
    k = w.shape[0]
    pad = (k - 1) // 2
    return lax.conv_general_dilated(
        u, w[:, None, :].astype(u.dtype), window_strides=(1,), padding=[(pad, pad)],
        dimension_numbers=('NWC', 'WIO', 'NWC'), feature_group_count=u.shape[-1])

def conv_mixers(u, w_in, conv_a, conv_b, conv_b_bias, ln_g, ln_b, w_out):
    p = u @ w_in
    gate_out, gate_in, val, glu_a, glu_g = jnp.split(
        p, [A_WIDTH, 2 * A_WIDTH, 3 * A_WIDTH, 3 * A_WIDTH + B_WIDTH], axis=-1)
    y_a = gate_out * depthwise_conv(gate_in * val, conv_a)
    z = depthwise_conv(glu_a * jax.nn.sigmoid(glu_g), conv_b) + conv_b_bias
    y_b = jax.nn.silu(layer_norm(z, ln_g, ln_b))
    return jnp.concatenate([y_a, y_b], axis=-1) @ w_out

def axial_rope_angles(seq_len):
    rows = seq_len // GRID_W
    row = jnp.repeat(jnp.arange(rows), GRID_W).astype(jnp.float32)
    col = jnp.tile(jnp.arange(GRID_W), rows).astype(jnp.float32)
    n_freq = C_HEAD_DIM // 4
    inv = ROPE_THETA ** (-jnp.arange(n_freq, dtype=jnp.float32) / n_freq)
    return row[:, None] * inv[None], col[:, None] * inv[None]

def rope_half(x, ang):
    cos = jnp.cos(ang)[None, :, None, None, :].astype(x.dtype)
    sin = jnp.sin(ang)[None, :, None, None, :].astype(x.dtype)
    x1, x2 = jnp.split(x, 2, axis=-1)
    return jnp.concatenate([x1 * cos - x2 * sin, x1 * sin + x2 * cos], axis=-1)

def axial_rope(x, ang_row, ang_col):
    xr, xc = jnp.split(x, 2, axis=-1)
    return jnp.concatenate([rope_half(xr, ang_row), rope_half(xc, ang_col)], axis=-1)

def split_q(p_q, g_q):
    b, l, _ = p_q.shape
    return rms_norm(p_q.reshape(b, l, C_HEADS, 2, C_HEAD_DIM), g_q)

def split_kv(p_kv, g_k):
    b, l, _ = p_kv.shape
    k, v = jnp.split(p_kv, [C_QK], axis=-1)
    k = rms_norm(k.reshape(b, l, C_HEADS, 2, C_HEAD_DIM), g_k)
    return k, v.reshape(b, l, C_HEADS, C_V_DIM)

def diff_attention(q, k, v, lam):
    s = jnp.einsum('bqhjd,bkhjd->bhjqk', q, k, preferred_element_type=jnp.float32) * (C_HEAD_DIM ** -0.5)
    p = jax.nn.softmax(s, axis=-1)
    a = p[:, :, 0] - lam * p[:, :, 1]
    return jnp.einsum('bhqk,bkhe->bqhe', a.astype(v.dtype), v)

def diff_attention_blocked(q, k, v, lam):
    b, l, h, _, dh = q.shape
    nb = l // Q_BLOCK
    qb = jnp.moveaxis(q.reshape(b, nb, Q_BLOCK, h, 2, dh), 1, 0)
    o = lax.map(lambda qi: diff_attention(qi, k, v, lam), qb)
    return jnp.moveaxis(o, 0, 1).reshape(b, l, h, C_V_DIM)

def diff_head_out(o, g_sub, lam_init):
    b, l = o.shape[:2]
    return (rms_norm(o, g_sub, SUBLN_EPS) * (1.0 - lam_init)).reshape(b, l, C_V)

def hyena_filter(seq_len, w1, b1, freq, w2, b2, w3):
    f32 = jnp.float32
    t = jnp.arange(seq_len, dtype=f32)
    t_unit = jnp.linspace(0.0, 1.0, seq_len)[:, None]
    bands = jnp.linspace(1e-4, HY_BANDS - 1, HY_BANDS)
    ang = (2.0 * math.pi / seq_len) * t[:, None] * bands[None]
    z = jnp.concatenate([t_unit, jnp.cos(ang), -jnp.sin(ang)], axis=-1)
    fr = freq.astype(f32)
    hid = jnp.sin(fr * (z @ w1.astype(f32) + b1.astype(f32)))
    hid = jnp.sin(fr * (hid @ w2.astype(f32) + b2.astype(f32)))
    h = hid @ w3.astype(f32)
    centre = seq_len // 2
    dist = jnp.abs(t - centre) / max(centre, 1)
    decay = jnp.abs(jnp.linspace(HY_MIN_DECAY, HY_MAX_DECAY, h.shape[-1]))
    return h * jnp.exp(-dist[:, None] * decay[None])

def fft_long_conv(u, h, bias):
    l = u.shape[1]
    n = 2 * l
    c0 = l // 2
    uf = jnp.fft.rfft(u.astype(jnp.float32), n=n, axis=1)
    hf = jnp.fft.rfft(h, n=n, axis=0)
    y = jnp.fft.irfft(uf * hf[None], n=n, axis=1)[:, c0:c0 + l]
    return (y + u.astype(jnp.float32) * bias.astype(jnp.float32)).astype(u.dtype)

def hyena_mixer(p_hy, conv_d, filt, bias):
    z = depthwise_conv(p_hy, conv_d)
    gate_out, gate_in, val = jnp.split(z, 3, axis=-1)
    return gate_out * fft_long_conv(gate_in * val, filt, bias)

def expert_choice_ffn(h, w_router, w_gate, w_up, w_down):
    b, n, d = h.shape
    cap = max(1, (EC_CAPACITY * n) // N_EXPERTS)
    aff = jax.nn.softmax((h @ w_router).astype(jnp.float32), axis=-1)
    g, idx = lax.top_k(jnp.swapaxes(aff, 1, 2), cap)
    xe = jax.vmap(lambda hb, ib: hb[ib])(h, idx)
    a = jnp.einsum('becd,edf->becf', xe, w_gate)
    up = jnp.einsum('becd,edf->becf', xe, w_up)
    y = jnp.einsum('becf,efd->becd', jax.nn.silu(a) * up, w_down) * g[..., None].astype(h.dtype)
    return jax.vmap(lambda ib, yb: jnp.zeros((n, d), h.dtype).at[ib.reshape(-1)].add(yb.reshape(-1, d)))(idx, y)

def first_inputs(seed: int = 0) -> dict:
    key = jax.random.key(seed)
    ks = iter(jax.random.split(key, 48))

    def nrm(shape, scale):
        return jax.random.normal(next(ks), shape, jnp.float32) * scale

    d = D_MODEL
    n_even = (DEPTH + 1) // 2
    n_odd = DEPTH // 2
    return {
        'x': nrm((BATCH, SEQ, d), 1.0),
        'c': nrm((BATCH, d), 1.0),
        'ctx': nrm((BATCH, CTX_LEN, d), 1.0),
        'c_ctx': nrm((d,), 1.0),
        'w_ada': nrm((DEPTH, d, 6 * d), 0.5 * d ** -0.5),
        'b_ada': nrm((DEPTH, 6 * d), 0.02),
        'g_mix': 1.0 + nrm((DEPTH, d), 0.1),
        'g_ffn': 1.0 + nrm((DEPTH, d), 0.1),
        'w_in_ab': nrm((n_even, d, AB_IN), d ** -0.5),
        'conv_a': nrm((n_even, SHORT_CONV_W, A_WIDTH), SHORT_CONV_W ** -0.5),
        'conv_b': nrm((n_even, CONFORMER_CONV_W, B_WIDTH), CONFORMER_CONV_W ** -0.5),
        'conv_b_bias': nrm((n_even, B_WIDTH), 0.02),
        'ln_b_g': 1.0 + nrm((n_even, B_WIDTH), 0.1),
        'ln_b_b': nrm((n_even, B_WIDTH), 0.02),
        'w_out_ab': nrm((n_even, MIX_WIDTH, d), MIX_WIDTH ** -0.5),
        'w_in_cd': nrm((n_odd, d, CD_IN), d ** -0.5),
        'g_q': 1.0 + nrm((n_odd, C_HEAD_DIM), 0.1),
        'g_k': 1.0 + nrm((n_odd, C_HEAD_DIM), 0.1),
        'lam_q1': nrm((n_odd, C_HEAD_DIM), 0.1),
        'lam_k1': nrm((n_odd, C_HEAD_DIM), 0.1),
        'lam_q2': nrm((n_odd, C_HEAD_DIM), 0.1),
        'lam_k2': nrm((n_odd, C_HEAD_DIM), 0.1),
        'g_subln': 1.0 + nrm((n_odd, C_V_DIM), 0.1),
        'conv_d': nrm((n_odd, SHORT_CONV_W, 3 * HY_WIDTH), SHORT_CONV_W ** -0.5),
        'hf_w1': nrm((n_odd, HY_EMB, HY_ORDER), HY_EMB ** -0.5),
        'hf_b1': nrm((n_odd, HY_ORDER), 0.1),
        'hf_freq': 1.0 + nrm((n_odd, HY_ORDER), 0.1),
        'hf_w2': nrm((n_odd, HY_ORDER, HY_ORDER), HY_ORDER ** -0.5),
        'hf_b2': nrm((n_odd, HY_ORDER), 0.1),
        'hf_w3': nrm((n_odd, HY_ORDER, HY_WIDTH), 0.02),
        'hf_bias': nrm((n_odd, HY_WIDTH), 0.1),
        'w_out_cd': nrm((n_odd, MIX_WIDTH, d), MIX_WIDTH ** -0.5),
        'w_router': nrm((DEPTH, d, N_EXPERTS), d ** -0.5),
        'w_gate': nrm((DEPTH, N_EXPERTS, d, EXPERT_FF), d ** -0.5),
        'w_up': nrm((DEPTH, N_EXPERTS, d, EXPERT_FF), d ** -0.5),
        'w_down': nrm((DEPTH, N_EXPERTS, EXPERT_FF, d), EXPERT_FF ** -0.5),
    }

def first_block(x, c, ctx, c_ctx, w_ada, b_ada, g_mix, g_ffn, w_in_ab, conv_a, conv_b, conv_b_bias,
              ln_b_g, ln_b_b, w_out_ab, w_in_cd, g_q, g_k, lam_q1, lam_k1, lam_q2, lam_k2, g_subln,
              conv_d, hf_w1, hf_b1, hf_freq, hf_w2, hf_b2, hf_w3, hf_bias, w_out_cd,
              w_router, w_gate, w_up, w_down):
    f32 = jnp.float32
    seq_lat = x.shape[1]
    seq_ctx = ctx.shape[1]
    ang_row, ang_col = axial_rope_angles(seq_lat)
    cond_lat = jax.nn.silu(c)
    cond_ctx = jax.nn.silu(c_ctx)[None]
    h_lat, h_ctx = x, ctx
    kv_cols = slice(C_QK, 2 * C_QK + C_V)
    hy_cols = slice(2 * C_QK + C_V, CD_IN)
    for l in range(DEPTH):
        last = l == DEPTH - 1
        odd = l % 2 == 1
        i = l // 2
        mod_lat = jnp.split((cond_lat @ w_ada[l] + b_ada[l])[:, None, :], 6, axis=-1)
        u_lat = modulate(rms_norm(h_lat, g_mix[l]), mod_lat[0], mod_lat[1])
        if odd or not last:
            mod_ctx = jnp.split((cond_ctx @ w_ada[l] + b_ada[l])[:, None, :], 6, axis=-1)
            u_ctx = modulate(rms_norm(h_ctx, g_mix[l]), mod_ctx[0], mod_ctx[1])
        if not odd:
            ab = (w_in_ab[i], conv_a[i], conv_b[i], conv_b_bias[i], ln_b_g[i], ln_b_b[i], w_out_ab[i])
            y_lat = conv_mixers(u_lat, *ab)
            if not last:
                y_ctx = conv_mixers(u_ctx, *ab)
        else:
            lam_init = 0.8 - 0.6 * math.exp(-0.3 * l)
            lam = (jnp.exp(jnp.sum(lam_q1[i].astype(f32) * lam_k1[i].astype(f32)))
                   - jnp.exp(jnp.sum(lam_q2[i].astype(f32) * lam_k2[i].astype(f32))) + lam_init)
            w_in = w_in_cd[i]
            p_lat = u_lat @ w_in
            q_l = axial_rope(split_q(p_lat[..., :C_QK], g_q[i]), ang_row, ang_col)
            k_l, v_l = split_kv(p_lat[..., kv_cols], g_k[i])
            k_l = axial_rope(k_l, ang_row, ang_col)
            if last:
                k_c, v_c = split_kv(u_ctx @ w_in[:, kv_cols], g_k[i])
            else:
                p_ctx = u_ctx @ w_in
                q_c = split_q(p_ctx[..., :C_QK], g_q[i])
                k_c, v_c = split_kv(p_ctx[..., kv_cols], g_k[i])
            k_all = jnp.concatenate([k_c, k_l], axis=1)
            v_all = jnp.concatenate([v_c, v_l], axis=1)
            o_lat = diff_attention_blocked(q_l, k_all, v_all, lam)
            filt_lat = hyena_filter(seq_lat, hf_w1[i], hf_b1[i], hf_freq[i], hf_w2[i], hf_b2[i], hf_w3[i])
            y_hy_lat = hyena_mixer(p_lat[..., hy_cols], conv_d[i], filt_lat, hf_bias[i])
            y_lat = jnp.concatenate([diff_head_out(o_lat, g_subln[i], lam_init), y_hy_lat], axis=-1) @ w_out_cd[i]
            if not last:
                o_ctx = diff_attention(q_c, k_c, v_c, lam)
                filt_ctx = hyena_filter(seq_ctx, hf_w1[i], hf_b1[i], hf_freq[i], hf_w2[i], hf_b2[i], hf_w3[i])
                y_hy_ctx = hyena_mixer(p_ctx[..., hy_cols], conv_d[i], filt_ctx, hf_bias[i])
                y_ctx = jnp.concatenate([diff_head_out(o_ctx, g_subln[i], lam_init), y_hy_ctx], axis=-1) @ w_out_cd[i]
        h_lat = h_lat + mod_lat[2] * y_lat
        u2 = modulate(rms_norm(h_lat, g_ffn[l]), mod_lat[3], mod_lat[4])
        h_lat = h_lat + mod_lat[5] * expert_choice_ffn(u2, w_router[l], w_gate[l], w_up[l], w_down[l])
        if not last:
            h_ctx = h_ctx + mod_ctx[2] * y_ctx
            u2c = modulate(rms_norm(h_ctx, g_ffn[l]), mod_ctx[3], mod_ctx[4])
            h_ctx = h_ctx + mod_ctx[5] * expert_choice_ffn(u2c, w_router[l], w_gate[l], w_up[l], w_down[l])
    return h_lat


NA_HEADS = 8
NA_HEAD_DIM = 64
NA_WIN_ROWS = 8
NA_WIN_COLS = 16
NA_QCOL_BLOCK = NA_WIN_COLS
NA_KCOL_BLOCK = 2 * NA_WIN_COLS
SW_HEADS = 8
SW_KV_HEADS = 2
SW_HEAD_DIM = 64
SW_WINDOW = 128
SW_BLOCK = 128
REL_BUCKETS = 32
REL_MAX_DIST = 128
D_FF = 2816
N_BRANCHES = 2
EPS = 1e-6
NEG = -1e30

NA_WIDTH = NA_HEADS * NA_HEAD_DIM
SW_Q_WIDTH = SW_HEADS * SW_HEAD_DIM
SW_KV_WIDTH = SW_KV_HEADS * SW_HEAD_DIM
IN_WIDTH = 3 * NA_WIDTH + SW_Q_WIDTH + 2 * SW_KV_WIDTH + N_BRANCHES * D_MODEL


def rms_norm_2(x, g):
    xf = x.astype(jnp.float32)
    y = xf * lax.rsqrt(jnp.mean(xf * xf, axis=-1, keepdims=True) + EPS)
    return (y * g.astype(jnp.float32)).astype(x.dtype)

def swiglu(x, w_gate, w_up, w_down):
    return (jax.nn.silu(x @ w_gate) * (x @ w_up)) @ w_down

def t5_bucket(rel):
    nb = REL_BUCKETS // 2
    max_exact = nb // 2
    n = np.abs(rel)
    large = max_exact + (np.log(np.maximum(n, 1) / max_exact)
                         / np.log(REL_MAX_DIST / max_exact) * (nb - max_exact)).astype(np.int32)
    large = np.minimum(large, nb - 1)
    return ((rel > 0) * nb + np.where(n < max_exact, n, large)).astype(np.int32)

def neighbourhood_attention(q, k, v, rpb):
    B, S, H, dh = q.shape
    rows = S // GRID_W
    kr = min(NA_WIN_ROWS, rows)
    ncb = GRID_W // NA_QCOL_BLOCK
    r = np.arange(rows)
    row_start = np.clip(r - kr // 2, 0, rows - kr)
    key_rows = row_start[:, None] + np.arange(kr)
    cb = np.arange(ncb)
    kcol_start = np.clip(cb * NA_QCOL_BLOCK - NA_WIN_COLS // 2, 0, GRID_W - NA_KCOL_BLOCK)
    key_cols = kcol_start[:, None] + np.arange(NA_KCOL_BLOCK)
    key_idx = (key_rows[:, None, :, None] * GRID_W + key_cols[None, :, None, :])
    key_idx = key_idx.reshape(rows, ncb, kr * NA_KCOL_BLOCK)
    kg = k[:, key_idx]
    vg = v[:, key_idx]
    qb = q.reshape(B, rows, ncb, NA_QCOL_BLOCK, H, dh)
    s = jnp.einsum('brcqhd,brckhd->bhrcqk', qb, kg).astype(jnp.float32) / math.sqrt(dh)
    q_cols = cb[:, None] * NA_QCOL_BLOCK + np.arange(NA_QCOL_BLOCK)
    q_col_start = np.clip(q_cols - NA_WIN_COLS // 2, 0, GRID_W - NA_WIN_COLS)
    kc = key_cols[:, None, :]
    col_ok = (kc >= q_col_start[..., None]) & (kc < q_col_start[..., None] + NA_WIN_COLS)
    row_idx = key_rows - r[:, None] + NA_WIN_ROWS - 1
    col_idx = np.clip(kc - q_cols[..., None] + NA_WIN_COLS - 1, 0, 2 * NA_WIN_COLS - 2)
    bias = rpb[:, row_idx[:, None, None, :, None], col_idx[None, :, :, None, :]]
    bias = bias.reshape(H, rows, ncb, NA_QCOL_BLOCK, kr * NA_KCOL_BLOCK)
    mask = np.broadcast_to(col_ok[None, :, :, None, :],
                           (rows, ncb, NA_QCOL_BLOCK, kr, NA_KCOL_BLOCK))
    mask = mask.reshape(rows, ncb, NA_QCOL_BLOCK, kr * NA_KCOL_BLOCK)
    s = jnp.where(mask, s + bias.astype(jnp.float32), NEG)
    p = jax.nn.softmax(s, axis=-1)
    o = jnp.einsum('bhrcqk,brckhd->brcqhd', p.astype(v.dtype), vg)
    return o.reshape(B, S, H * dh)

def sliding_window_gqa(q, k, v, rel_bias, sink):
    B, S, _, dh = q.shape
    nb = S // SW_BLOCK
    rep = SW_HEADS // SW_KV_HEADS
    qb = q.reshape(B, nb, SW_BLOCK, SW_KV_HEADS, rep, dh)
    pad = ((0, 0), (SW_BLOCK, SW_BLOCK), (0, 0), (0, 0))
    kp = jnp.pad(k, pad).reshape(B, nb + 2, SW_BLOCK, SW_KV_HEADS, dh)
    vp = jnp.pad(v, pad).reshape(B, nb + 2, SW_BLOCK, SW_KV_HEADS, dh)
    kb = jnp.concatenate([kp[:, :-2], kp[:, 1:-1], kp[:, 2:]], axis=2)
    vb = jnp.concatenate([vp[:, :-2], vp[:, 1:-1], vp[:, 2:]], axis=2)
    s = jnp.einsum('bnqgrd,bnkgd->bgrnqk', qb, kb).astype(jnp.float32) / math.sqrt(dh)
    a = np.arange(SW_BLOCK)[:, None]
    j = np.arange(3 * SW_BLOCK)[None, :]
    rel = j - SW_BLOCK - a
    kpos = (np.arange(nb)[:, None, None] - 1) * SW_BLOCK + j[None]
    mask = (np.abs(rel)[None] <= SW_WINDOW) & (kpos >= 0) & (kpos < S)
    bias = rel_bias.astype(jnp.float32).reshape(SW_KV_HEADS, rep, 1, SW_BLOCK, 3 * SW_BLOCK)
    s = jnp.where(mask, s + bias, NEG)
    sink_b = sink.astype(jnp.float32).reshape(SW_KV_HEADS, rep, 1, 1, 1)
    m = jnp.maximum(s.max(axis=-1, keepdims=True), sink_b)
    e = jnp.exp(s - m)
    p = e / (e.sum(axis=-1, keepdims=True) + jnp.exp(sink_b - m))
    o = jnp.einsum('bgrnqk,bnkgd->bnqgrd', p.astype(v.dtype), vb)
    return o.reshape(B, S, SW_HEADS * dh)

def second_inputs(seed: int = 0) -> dict:
    key = jax.random.key(seed)
    ks = jax.random.split(key, 24)
    L, D, F = DEPTH, D_MODEL, D_FF
    nrm = lambda k, shape, fan: jax.random.normal(k, shape, jnp.float32) * fan ** -0.5
    gain = lambda k, shape: 1.0 + 0.05 * jax.random.normal(k, shape, jnp.float32)
    return {
        "x": jax.random.normal(ks[0], (BATCH, SEQ, D), jnp.float32),
        "ffn1_norm": gain(ks[1], (L, D)),
        "ffn1_w_gate": nrm(ks[2], (L, D, F), D),
        "ffn1_w_up": nrm(ks[3], (L, D, F), D),
        "ffn1_w_down": nrm(ks[4], (L, F, D), F),
        "mix_norm": gain(ks[5], (L, D)),
        "w_in": nrm(ks[6], (L, D, IN_WIDTH), D),
        "b_gate": 0.01 * jax.random.normal(ks[7], (L, N_BRANCHES * D), jnp.float32),
        "na_q_norm": gain(ks[8], (L, NA_HEAD_DIM)),
        "na_k_norm": gain(ks[9], (L, NA_HEAD_DIM)),
        "na_rpb": 0.1 * jax.random.normal(ks[10], (L, NA_HEADS, 2 * NA_WIN_ROWS - 1, 2 * NA_WIN_COLS - 1), jnp.float32),
        "sw_q_norm": gain(ks[11], (L, SW_HEAD_DIM)),
        "sw_k_norm": gain(ks[12], (L, SW_HEAD_DIM)),
        "sw_sink": 0.5 * jax.random.normal(ks[13], (L, SW_HEADS), jnp.float32),
        "t5_rel_table": 0.1 * jax.random.normal(ks[14], (REL_BUCKETS, SW_HEADS), jnp.float32),
        "w_branch_na": nrm(ks[15], (L, NA_WIDTH, D), NA_WIDTH),
        "w_branch_sw": nrm(ks[16], (L, SW_Q_WIDTH, D), SW_Q_WIDTH),
        "w_out": nrm(ks[17], (L, D, D), D),
        "ffn2_norm": gain(ks[18], (L, D)),
        "ffn2_w_gate": nrm(ks[19], (L, D, F), D),
        "ffn2_w_up": nrm(ks[20], (L, D, F), D),
        "ffn2_w_down": nrm(ks[21], (L, F, D), F),
    }

def second_block(x, ffn1_norm, ffn1_w_gate, ffn1_w_up, ffn1_w_down, mix_norm, w_in, b_gate,
              na_q_norm, na_k_norm, na_rpb, sw_q_norm, sw_k_norm, sw_sink, t5_rel_table,
              w_branch_na, w_branch_sw, w_out, ffn2_norm, ffn2_w_gate, ffn2_w_up, ffn2_w_down):
    B, S, D = x.shape
    rel = np.arange(3 * SW_BLOCK)[None, :] - SW_BLOCK - np.arange(SW_BLOCK)[:, None]
    t5_bias = jnp.transpose(t5_rel_table[t5_bucket(rel)], (2, 0, 1))
    splits = np.cumsum([NA_WIDTH, NA_WIDTH, NA_WIDTH, SW_Q_WIDTH, SW_KV_WIDTH, SW_KV_WIDTH])
    for l in range(DEPTH):
        x = x + 0.5 * swiglu(rms_norm_2(x, ffn1_norm[l]), ffn1_w_gate[l], ffn1_w_up[l], ffn1_w_down[l])
        h = rms_norm_2(x, mix_norm[l])
        z = h @ w_in[l]
        qa, ka, va, qs, ks_, vs, zg = jnp.split(z, splits, axis=-1)
        qa = rms_norm_2(qa.reshape(B, S, NA_HEADS, NA_HEAD_DIM), na_q_norm[l])
        ka = rms_norm_2(ka.reshape(B, S, NA_HEADS, NA_HEAD_DIM), na_k_norm[l])
        va = va.reshape(B, S, NA_HEADS, NA_HEAD_DIM)
        o_na = neighbourhood_attention(qa, ka, va, na_rpb[l])
        qs = rms_norm_2(qs.reshape(B, S, SW_HEADS, SW_HEAD_DIM), sw_q_norm[l])
        ks_ = rms_norm_2(ks_.reshape(B, S, SW_KV_HEADS, SW_HEAD_DIM), sw_k_norm[l])
        vs = vs.reshape(B, S, SW_KV_HEADS, SW_HEAD_DIM)
        o_sw = sliding_window_gqa(qs, ks_, vs, t5_bias, sw_sink[l])
        g = jax.nn.sigmoid((zg + b_gate[l]).astype(jnp.float32)).astype(x.dtype)
        g = g.reshape(B, S, N_BRANCHES, D)
        merged = g[:, :, 0] * (o_na @ w_branch_na[l]) + g[:, :, 1] * (o_sw @ w_branch_sw[l])
        x = x + merged @ w_out[l]
        x = x + 0.5 * swiglu(rms_norm_2(x, ffn2_norm[l]), ffn2_w_gate[l], ffn2_w_up[l], ffn2_w_down[l])
    return x


def setup_inputs(seed=0):
    out = dict(first_inputs(seed))
    for name, value in second_inputs(seed + 1).items():
        if name != "x":
            out[name + "_2"] = value
    return out


def reference(
    x, c, ctx, c_ctx, w_ada, b_ada, g_mix, g_ffn, w_in_ab, conv_a, conv_b, conv_b_bias, ln_b_g,
    ln_b_b, w_out_ab, w_in_cd, g_q, g_k, lam_q1, lam_k1, lam_q2, lam_k2, g_subln, conv_d, hf_w1,
    hf_b1, hf_freq, hf_w2, hf_b2, hf_w3, hf_bias, w_out_cd, w_router, w_gate, w_up, w_down,
    ffn1_norm_2, ffn1_w_gate_2, ffn1_w_up_2, ffn1_w_down_2, mix_norm_2, w_in_2, b_gate_2,
    na_q_norm_2, na_k_norm_2, na_rpb_2, sw_q_norm_2, sw_k_norm_2, sw_sink_2, t5_rel_table_2,
    w_branch_na_2, w_branch_sw_2, w_out_2, ffn2_norm_2, ffn2_w_gate_2, ffn2_w_up_2,
    ffn2_w_down_2,
):
    x = first_block(
        x, c, ctx, c_ctx, w_ada, b_ada, g_mix, g_ffn, w_in_ab, conv_a, conv_b, conv_b_bias,
        ln_b_g, ln_b_b, w_out_ab, w_in_cd, g_q, g_k, lam_q1, lam_k1, lam_q2, lam_k2, g_subln,
        conv_d, hf_w1, hf_b1, hf_freq, hf_w2, hf_b2, hf_w3, hf_bias, w_out_cd, w_router, w_gate,
        w_up, w_down,
    )
    return second_block(
        x, ffn1_norm_2, ffn1_w_gate_2, ffn1_w_up_2, ffn1_w_down_2, mix_norm_2, w_in_2, b_gate_2,
        na_q_norm_2, na_k_norm_2, na_rpb_2, sw_q_norm_2, sw_k_norm_2, sw_sink_2, t5_rel_table_2,
        w_branch_na_2, w_branch_sw_2, w_out_2, ffn2_norm_2, ffn2_w_gate_2, ffn2_w_up_2,
        ffn2_w_down_2,
    )


_drawn_inputs = setup_inputs


def setup_inputs(seed=0):
    import zlib

    import numpy as np

    out = dict(_drawn_inputs(seed))
    spreads = {}
    factors = {'conv_b_bias': 7.278,
     'ln_b_g': 2.731,
     'ln_b_b': 8.0,
     'g_q': 4.969,
     'g_k': 5.701,
     'lam_q2': 8.0,
     'lam_k2': 6.277,
     'g_subln': 3.351,
     'hf_b1': 3.569,
     'hf_freq': 4.902,
     'hf_b2': 2.731,
     'mix_norm_2': 3.719,
     'b_gate_2': 8.0,
     'na_q_norm_2': 8.0,
     'na_k_norm_2': 8.0,
     'na_rpb_2': 4.141,
     'sw_q_norm_2': 8.0,
     'sw_k_norm_2': 8.0,
     'sw_sink_2': 8.0,
     't5_rel_table_2': 8.0}
    for name, (base, spread) in spreads.items():
        noise = np.random.default_rng([zlib.crc32(name.encode()), seed]).standard_normal(out[name].shape)
        drawn = base * np.exp(spread * noise) if base else spread * noise
        out[name] = jnp.asarray(drawn.astype(out[name].dtype))
    for name, factor in factors.items():
        out[name] = (out[name] * factor).astype(out[name].dtype)
    return out
```

```python
import math
from contextlib import contextmanager

import numpy as np

import concourse.bass as bass
from concourse import mybir

F32 = mybir.dt.float32
ACT = mybir.ActivationFunctionType
ALU = mybir.AluOpType
AX = mybir.AxisListType
ET = mybir.EngineType

P = 128
D = 1024
KB = D // P
T = 256
NS = 2
TT = T // P
AW = 512
JB = AW // P
HEADS = 4
NE, CAP = 16, 32
EG = 4
TAPS_A, TAPS_B = 3, 31
FF = 2816
FB = FF // P
GRID = 64
ROWS = T // GRID
NA_H, SW_H, DH = 8, 8, 64
RPB_R, RPB_C = 15, 31
EPS, SUB_EPS = 1e-6, 1e-5
LAM_INIT = 0.8 - 0.6 * math.exp(-0.3)
NEG = -1e30
TWO_PI = 2.0 * math.pi
ROUND = 1.5 * 2.0 ** 23
SLOTS, SLOT = 12, 2048
ARENA = 18432
LAYERS = 2


def columns(*names):
    at, out = 0, {}
    for name, n in names:
        out[name] = (at, n)
        at += n
    return out, at


VEC, NVEC = columns(("c", KB), ("c_ctx", KB), ("b_ada", 2 * 6 * KB), ("g_mix", 2 * KB), ("g_ffn", 2 * KB),
                    ("conv_a", TAPS_A * JB), ("conv_b", TAPS_B * JB), ("conv_b_bias", JB), ("ln_b_g", JB),
                    ("ln_b_b", JB), ("g_q", 1), ("g_k", 1), ("lam_q1", 1), ("lam_q2", 1), ("lam_k1", 1),
                    ("lam_k2", 1), ("g_subln", 1), ("conv_d", 3 * 3 * JB), ("hf_bias", JB), ("hf_b1", 1),
                    ("hf_freq", 1), ("hf_b2", 1), ("w_router", 2 * KB * NE))
LVEC, NLVEC = columns(("ffn1_norm", KB), ("mix_norm", KB), ("ffn2_norm", KB), ("b_gate", 2 * KB),
                      ("na_q_norm", 1), ("na_k_norm", 1), ("sw_q_norm", 1), ("sw_k_norm", 1))
KEPT, NKEPT = columns(("ident", P), ("ones", P), ("halves", P), ("rope_swap", P), ("slot_no", CAP))
EARLY, NEARLY = columns(("z", T), ("decay", TT * AW), ("dft", TT * 2 * T))
MIDDLE, NMIDDLE = columns(("cos", T), ("sin", T), ("idft", 4 * T))
LATE, NLATE = columns(("na_mask", TT * T), ("sw_mask", TT * T), ("bucket", 2 * T))


def blocks(v):
    return np.ascontiguousarray(v.reshape(-1, P).T)


def padded(v):
    out = np.zeros((P, v.shape[1]), np.float32)
    out[:v.shape[0]] = v
    return out


def twice(v):
    return np.concatenate([v, v]).reshape(P, 1)


def pack_vectors(a):
    col = {"c": blocks(a["c"]), "c_ctx": blocks(a["c_ctx"]), "b_ada": blocks(a["b_ada"]),
           "g_mix": blocks(a["g_mix"]), "g_ffn": blocks(a["g_ffn"]), "conv_a": blocks(a["conv_a"]),
           "conv_b": blocks(a["conv_b"]), "conv_b_bias": blocks(a["conv_b_bias"]), "ln_b_g": blocks(a["ln_b_g"]),
           "ln_b_b": blocks(a["ln_b_b"]), "g_q": twice(a["g_q"][0]), "g_k": twice(a["g_k"][0]),
           "g_subln": blocks(a["g_subln"]), "conv_d": blocks(a["conv_d"]), "hf_bias": blocks(a["hf_bias"])}
    for n in ("lam_q1", "lam_q2", "lam_k1", "lam_k2", "hf_b1", "hf_freq", "hf_b2"):
        col[n] = padded(a[n][0].reshape(-1, 1))
    col["w_router"] = a["w_router"].reshape(2, KB, P, NE).transpose(2, 0, 1, 3).reshape(P, -1)
    return np.ascontiguousarray(np.concatenate([col[n] for n in VEC], axis=1))


def pack_layer_vectors(a):
    lots = []
    for l in range(LAYERS):
        col = {n: blocks(a[n + "_2"][l]) for n in ("ffn1_norm", "mix_norm", "ffn2_norm", "b_gate")}
        col |= {n: twice(a[n + "_2"][l]) for n in ("na_q_norm", "na_k_norm", "sw_q_norm", "sw_k_norm")}
        lots.append(np.concatenate([col[n] for n in LVEC], axis=1))
    return np.ascontiguousarray(np.concatenate(lots, axis=1))


def by_rows(m):
    n = m.shape[0] // P
    return m.reshape(n, P, -1).transpose(1, 0, 2).reshape(P, -1)


def kept_constants():
    halves = np.kron(np.eye(2), np.ones((DH, DH)))
    swap = np.zeros((P, P))
    for f in range(P):
        swap[f ^ 16, f] = 1.0
    slot_no = np.tile(np.arange(CAP), (P, 1))
    return np.concatenate([np.eye(P), np.ones((P, P)), halves, swap, slot_no], axis=1).astype(np.float32)


def early_constants():
    f32 = np.float32
    t = np.arange(T, dtype=f32)
    bands = np.linspace(1e-4, 15, 16, dtype=f32)
    ang = ((f32(TWO_PI / T) * t)[:, None] * bands[None]).astype(np.float64)
    z = np.concatenate([np.linspace(0.0, 1.0, T)[:, None], np.cos(ang), -np.sin(ang)], axis=1)
    dist = np.abs(t - T // 2) / (T // 2)
    rate = np.abs(np.linspace(math.log(1e-2) / 1.5, math.log(1e-2) / 0.3, AW))
    decay = np.exp(-dist[:, None].astype(np.float64) * rate[None])
    ph = np.pi * np.outer(np.arange(T), np.arange(T) + 0.5) / T
    dft = np.concatenate([np.cos(ph), -np.sin(ph)], axis=1)
    return np.concatenate([padded(z.T), by_rows(decay), by_rows(dft)], axis=1).astype(f32)


def middle_constants():
    f32 = np.float32
    inv = (f32(10000.0) ** (-np.arange(16, dtype=f32) / f32(16))).astype(f32)
    tok = np.arange(T)
    row, col = (tok // GRID).astype(f32), (tok % GRID).astype(f32)
    f = np.arange(P) % DH
    ang = np.where((f < 32)[:, None], row[None], col[None]).astype(f32) * inv[f % 16][:, None]
    ang = ang.astype(f32).astype(np.float64)
    cos, sin = np.cos(ang), np.sin(ang) * np.where((f % 32 < 16), -1.0, 1.0)[:, None]
    ph = np.pi * np.outer(np.arange(T) + 0.5, np.arange(T) + T // 2) / T
    idft = np.concatenate([np.cos(ph), -np.sin(ph)], axis=0) / T
    return np.concatenate([cos, sin, by_rows(idft)], axis=1).astype(f32)


def late_constants():
    q, k = np.arange(T)[:, None], np.arange(T)[None]
    start = np.clip(q % GRID - 8, 0, GRID - 16)
    na = np.where((k % GRID >= start) & (k % GRID < start + 16), 0.0, NEG)
    sw = np.where(np.abs(k - q) <= P, 0.0, NEG)
    rel = np.arange(2 * T) - (T - 1)
    n = np.abs(rel)
    large = np.minimum(8 + (np.log(np.maximum(n, 1) / 8) / np.log(128 / 8) * 8).astype(np.int32), 15)
    bucket = (rel > 0) * 16 + np.where(n < 8, n, large)
    hot = (np.arange(32)[:, None] == bucket[None]).astype(np.float32)
    return np.concatenate([by_rows(na)[::-1], by_rows(sw)[::-1], padded(hot)], axis=1).astype(np.float32)


class Count:

    def __init__(self, nc, name, unit=1):
        self.name, self.unit, self.n, self.loop = name, unit, 0, None
        self.sem = nc.alloc_semaphore(name)

    def step(self, ins, steps=1):
        ins.then_inc(self.sem, self.unit * steps)
        self.n += steps
        return self.here()

    def here(self):
        return Mark(self, self.n, self.loop)


class Mark:

    def __init__(self, count, n, loop=None):
        self.count, self.n, self.loop = count, n, loop

    def value(self, turn=None):
        steps = self.n if self.loop is None else self.n + self.loop.stride[self.count.name] * turn
        return steps * self.count.unit


class Loop:

    def __init__(self, name, turns, stride):
        self.name, self.turns, self.stride, self.made = name, turns, stride, {}


class Queue:

    def __init__(self, nc, eng, name):
        self.eng, self.name = eng, name
        self.count = Count(nc, f"{name}_done")
        self.counts = [self.count]
        self.past, self.past_turn = {}, {}
        self.turn, self.loop = None, None

    def after(self, *marks, turn=None):
        for m in marks:
            if m is None:
                continue
            if isinstance(m, (list, tuple)):
                self.after(*m, turn=turn)
                continue
            if m.loop is None:
                v = m.value()
                if v == 0:
                    continue
                if self.past.get(m.count, 0) >= v or (m.count in self.past_turn):
                    continue
                self.past[m.count] = v
            elif turn is not None:
                v = m.value(turn)
            elif m.loop is self.loop:
                if self.past_turn.get(m.count, 0) >= m.n:
                    continue
                self.past_turn[m.count] = m.n
                v = m.value(self.turn)
            else:
                v = m.value(m.loop.turns - 1)
                if self.past.get(m.count, 0) >= v:
                    continue
                self.past[m.count] = v
            self.eng.wait_ge(m.count.sem, v)

    def done(self, ins):
        return self.count.step(ins)

    def last(self):
        return [c.here() for c in self.counts]


@contextmanager
def turns_of(nc, name, turns, queues, counts, known, made):
    loop = Loop(name, turns, known.get(name) or {c.name: 1 for c in counts})
    base = {c: c.n for c in counts}
    engines = tuple({"pe": ET.PE, "act": ET.Activation, "dve": ET.DVE, "pool": ET.Pool,
                     "sp": ET.SP}[q.name] for q in queues)
    for c in counts:
        c.loop = loop
    with nc.Fori(0, turns, engines=engines) as i:
        for q in queues:
            q.turn, q.loop, q.past_turn = i, loop, {}
        yield loop, i
        for q in queues:
            q.turn, q.loop, q.past_turn = None, None, {}
    loop.stride = made[name] = {c.name: c.n - base[c] for c in counts}
    for c in counts:
        c.loop = None
        c.n = base[c] + loop.stride[c.name] * turns


def program(nc, a, out, known):
    made = {}

    def hold(name, floats):
        return nc.alloc_sbuf_tensor(f"sb_{name}", [P, floats], F32)

    pe, act, dve = Queue(nc, nc.tensor, "pe"), Queue(nc, nc.scalar, "act"), Queue(nc, nc.vector, "dve")
    pool, sp = Queue(nc, nc.gpsimd, "pool"), Queue(nc, nc.sync, "sp")
    workers = [pe, act, dve, pool]

    ring = hold("ring", SLOTS * SLOT)
    H = hold("hidden", NS * KB * T)[:, :].rearrange("p (s k t) -> p s k t", s=NS, k=KB)
    U = hold("normed", NS * KB * T)[:, :].rearrange("p (s k t) -> p s k t", s=NS, k=KB)
    vec_mem, kept_mem = hold("vectors", NVEC), hold("kept", NKEPT)
    lvec_mem, cur = hold("layer_vectors", LAYERS * NLVEC), hold("layer_now", NLVEC)
    sink_mem = hold("sinks", LAYERS * SW_H)
    mod_mem = hold("modulation", 2 * 6 * KB * NS)
    MOD = mod_mem[:, :].rearrange("p (l c k s) -> p l c k s", l=2, c=6, k=KB)
    fold_mem = hold("folded_gains", 2 * 2 * KB * NS)
    FOLD = fold_mem[:, :].rearrange("p (l n k s) -> p l n k s", l=2, n=2, k=KB)
    small = hold("small", 256)
    arena = hold("arena", ARENA)
    banks = [nc.alloc_psum_tensor(f"bank{b}", [P, 512], F32) for b in range(8)]
    bank_read = [None] * 8

    def vec(name, i=0, n=1):
        c = VEC[name][0] + i
        return vec_mem[:, c:c + n]

    def kept(name):
        c, n = KEPT[name]
        return kept_mem[:, c:c + n]

    ident, ones, halves = kept("ident"), kept("ones"), kept("halves")

    class Carve:

        def __init__(self, at=0, end=ARENA, mem=None):
            self.at, self.end, self.mem = at, end, arena[:, :] if mem is None else mem

        def __call__(self, *shape):
            n = math.prod(shape)
            self.at += n
            assert self.at <= self.end, (self.at, self.end)
            part = self.mem[:, self.at - n:self.at]
            if len(shape) == 1:
                return part
            names = "abcd"[:len(shape)]
            return part.rearrange(f"p ({' '.join(names)}) -> p {' '.join(names)}", **dict(zip(names, shape)))

    landed = [Count(nc, f"landed{s}", 16) for s in range(SLOTS)]
    chunks_read = Count(nc, "chunks_read")
    pe.counts.append(chunks_read)
    issued = [0]

    def fetch(src):
        slot, k = issued[0] % SLOTS, src.shape[0] // P
        issued[0] += 1
        if issued[0] > SLOTS:
            sp.after(Mark(chunks_read, issued[0] - SLOTS, chunks_read.loop))
        tile = ring[:, slot * SLOT:(slot + 1) * SLOT].rearrange("p (k n) -> p k n", k=k)
        return tile, landed[slot].step(nc.sync.dma_start(tile, src.rearrange("(k p) n -> p k n", p=P)))

    def meet(*queues):
        marks = [q.last() for q in workers]
        for q in queues or workers:
            q.after(marks)

    def mm(o, lhsT, rhs, start, stop):
        return nc.tensor.matmul(o, lhsT, rhs, start=start, stop=stop, skip_group_check=True)

    def turn_over(o, x, *marks):
        pe.after(*marks)
        return nc.tensor.transpose(o, x, ident[0:x.shape[0], 0:x.shape[0]])

    def A(o, x, func, *marks, bias=None, scale=None, accum=None):
        act.after(*marks)
        kw = {}
        if bias is not None:
            kw["bias"] = bias
        if scale is not None:
            kw["scale"] = scale
        if accum is not None:
            kw["accum_out"] = accum
        return act.done(nc.scalar.activation(o, x, func, **kw))

    def copy_a(o, x, *marks):
        act.after(*marks)
        return act.done(nc.scalar.copy(o, x))

    def copy_v(o, x, *marks):
        dve.after(*marks)
        return dve.done(nc.vector.tensor_copy(o, x))

    def TS(o, x, s1, op0, s2=None, op1=None, marks=()):
        dve.after(*marks)
        if s2 is None:
            return dve.done(nc.vector.tensor_scalar(o, x, s1, None, op0))
        return dve.done(nc.vector.tensor_scalar(o, x, s1, s2, op0, op1))

    def STT(o, x, s, y, op0, op1, marks=()):
        dve.after(*marks)
        return dve.done(nc.vector.scalar_tensor_tensor(out=o, in0=x, scalar=s, in1=y, op0=op0, op1=op1))

    def VV(o, x, y, op, marks=()):
        dve.after(*marks)
        return dve.done(nc.vector.tensor_tensor(o, x, y, op))

    def RED(o, x, op, marks=(), negate=False):
        dve.after(*marks)
        return dve.done(nc.vector.tensor_reduce(o, x, AX.X, op, negate=negate))

    def RECIP(o, x, *marks):
        dve.after(*marks)
        return dve.done(nc.vector.reciprocal(o, x))

    def fill(o, value, *marks):
        dve.after(*marks)
        return dve.done(nc.vector.memset(o, value))

    def load(count, dst, src, q=act, after=()):
        q.after(*after)
        return count.step(q.eng.dma_start(dst, src))

    def counted(name):
        return Count(nc, name, 16)

    m_vec = load(counted("in_vectors"), vec_mem[:, :], a["vectors"])
    m_kept = load(counted("in_kept"), kept_mem[:, :], a["kept"])
    low = Carve()
    cond, ada_row = low(KB, CAP), low(512)
    carve = Carve(low.at)
    top = Carve(ARENA - NMIDDLE - 2048 - TT * 2 * T)
    BLOCK1_END = top.at
    dft = top(TT, 2 * T)
    HF = top(4, AW)
    COS, SIN, idft = top(T), top(T), top(4, T)
    m_x = load(counted("in_x"), H[:, 0], a["x_t"].rearrange("(k p) t -> p k t", p=P))
    m_ctx = load(counted("in_ctx"), H[:, 1], a["ctx_t"].rearrange("(k p) t -> p k t", p=P))
    z, decay = carve(T), carve(TT, AW)
    fw1, fw2, fw3 = carve(64), carve(64), carve(AW)
    e = EARLY["decay"][0], EARLY["dft"][0]
    in_filter = counted("in_filter")
    load(in_filter, fw1[0:33, :], a["hf_w1"][0])
    load(in_filter, fw2[0:64, :], a["hf_w2"][0])
    load(in_filter, fw3[0:64, :], a["hf_w3"][0])
    load(in_filter, z, a["early"][:, 0:e[0]])
    load(in_filter, decay.rearrange("p t n -> p (t n)"), a["early"][:, e[0]:e[1]])
    m_filter = load(in_filter, dft.rearrange("p t n -> p (t n)"), a["early"][:, e[1]:])
    in_middle = counted("in_middle")
    load(in_middle, COS, a["middle"][:, 0:T])
    load(in_middle, SIN, a["middle"][:, T:2 * T])
    m_middle = load(in_middle, idft.rearrange("p b t -> p (b t)"), a["middle"][:, 2 * T:])
    in_layers = counted("in_layer_vectors")
    load(in_layers, lvec_mem[:, :], a["layer_vectors"])
    m_layers = load(in_layers, sink_mem[:, :], bass.AP(tensor=a["sw_sink_2"].tensor, offset=0,
                                                        ap=[[0, P], [1, LAYERS * SW_H]]))

    m = fill(cond, 0.0)
    A(cond[:, :, 0], vec("c", 0, KB), ACT.Silu, m, m_vec)
    m_cond = A(cond[:, :, 1], vec("c_ctx", 0, KB), ACT.Silu)
    ADA_BANK, TURN_BANK = 6, 7

    def ada(l, pair):
        bank = banks[ADA_BANK]
        pe.after(m_cond)
        pe.after(bank_read[ADA_BANK])
        for h in range(2):
            c0 = D * (2 * pair + h)
            for r in range(KB // 2):
                w, there = fetch(a["w_ada"][l, 2 * P * r:2 * P * (r + 1), c0:c0 + D])
                pe.after(there)
                for kk in range(2):
                    k = 2 * r + kk
                    for half in range(2):
                        j = 2 * h + half
                        ins = mm(bank[32 * j:32 * j + 32, :], cond[:, k, :],
                                 w[:, kk, 512 * half:512 * half + 512], k == 0, k == KB - 1)
                m = chunks_read.step(ins)
        m = bank_read[ADA_BANK] = copy_a(ada_row, bank[:, :], m)
        pe.after(bank_read[TURN_BANK])
        for c in range(4):
            ins = turn_over(banks[TURN_BANK][:, P * c:P * c + P], ada_row[:, P * c:P * c + P], m, m_kept)
        m = pe.done(ins)
        turned = banks[TURN_BANK][:, :].rearrange("p (c m) -> p c m", c=4)
        for j in range(4):
            sec, k = 2 * pair + j // 2, 4 * (j % 2)
            bias = vec("b_ada", (l * 6 + sec) * KB + k, 4).rearrange("p (k o) -> p k o", o=1).broadcast_to([P, 4, NS])
            done = VV(MOD[:, l, sec, k:k + 4, :], turned[:, :, 32 * j:32 * j + NS], bias, ALU.add, marks=[m, m_vec])
        bank_read[TURN_BANK] = done
        return done

    def fold(l, n, m):
        g = vec("g_ffn" if n else "g_mix", l * KB, KB)
        for s in range(NS):
            m = STT(FOLD[:, l, n, :, s], MOD[:, l, 3 * n + 1, :, s], 1.0, g, ALU.add, ALU.mult, marks=[m])
        return m

    turns, arg, hid = carve(T), carve(T), carve(T)
    htok = carve(TT, AW)

    def sine(o, x, m):
        hi = 6.28125
        m = TS(turns[0:64, :], x, 1.0 / TWO_PI, ALU.mult, ROUND, ALU.add, marks=[m])
        m = TS(turns[0:64, :], turns[0:64, :], ROUND, ALU.subtract, marks=[m])
        m = STT(x, turns[0:64, :], -hi, x, ALU.mult, ALU.add, marks=[m])
        m = STT(x, turns[0:64, :], hi - TWO_PI, x, ALU.mult, ALU.add, marks=[m])
        m = TS(x, x, 3.1415925, ALU.min, -3.1415925, ALU.max, marks=[m])
        return A(o, x, ACT.Sin, m)

    freq = vec("hf_freq")[0:64, :]
    pe.after(m_filter)
    m = pe.done(mm(banks[0][0:64, 0:T], fw1[0:33, 0:64], z[0:33, :], True, True))
    m = TS(arg[0:64, :], banks[0][0:64, 0:T], vec("hf_b1")[0:64, :], ALU.add, freq, ALU.mult, marks=[m, m_vec])
    m = sine(hid[0:64, :], arg[0:64, :], m)
    pe.after(m)
    m = pe.done(mm(banks[1][0:64, 0:T], fw2[0:64, 0:64], hid[0:64, :], True, True))
    m = TS(arg[0:64, :], banks[1][0:64, 0:T], vec("hf_b2")[0:64, :], ALU.add, freq, ALU.mult, marks=[m])
    m = sine(hid[0:64, :], arg[0:64, :], m)
    pe.after(m)
    for t in range(TT):
        m = pe.done(mm(banks[2 + t][:, :], hid[0:64, t * P:t * P + P], fw3[0:64, :], True, True))
        m = VV(htok[:, t, :], banks[2 + t][:, :], decay[:, t, :], ALU.mult, marks=[m, m_filter])
    pe.after(m)
    for b in range(4):
        for t in range(TT):
            ins = mm(banks[b][:, :], dft[:, t, b * P:b * P + P], htok[:, t, :], t == 0, t == TT - 1)
        copy_a(HF[:, b, :], banks[b][:, :], pe.done(ins))

    def inverse_rms(o, total, scale, eps, m):
        m = TS(o, total, scale, ALU.mult, eps, ALU.add, marks=[m])
        m = RECIP(o, o, m)
        return m, A(o, o, ACT.Sqrt, m)

    def rms(b, streams, sq, rinv):
        w, lo, read = len(streams) * T, streams[0], [None, None]
        pe.after(bank_read[b])
        for k in range(KB):
            part = sq[:, 512 * (k % 2):512 * (k % 2) + w]
            pe.after(A(part.rearrange("p (s t) -> p s t", t=T), H[:, lo:lo + len(streams), k, :], ACT.Square,
                       read[k % 2]))
            read[k % 2] = pe.done(mm(banks[b][:, 0:w], ones, part, k == 0, k == KB - 1))
        bank_read[b], m = inverse_rms(rinv[:, 0:w], banks[b][:, 0:w], 1.0 / D, EPS, read[(KB - 1) % 2])
        return m

    def modulated(l, n, streams, b, sq, rinv):
        m = rms(b, streams, sq, rinv)
        out = []
        for k in range(KB):
            for i, s in enumerate(streams):
                v = STT(U[:, s, k, :], H[:, s, k, :], FOLD[:, l, n, k, s:s + 1], rinv[:, i * T:i * T + T],
                        ALU.mult, ALU.mult, marks=[m])
                v = A(U[:, s, k, :], U[:, s, k, :], ACT.Identity, v, bias=MOD[:, l, 3 * n, k, s:s + 1])
            out.append(v)
        return out

    def columns_of(w, c0, n=SLOT // KB):
        return w[:, c0:c0 + n]

    m = fold(0, 0, ada(0, 0))
    meet()
    carve = Carve(low.at, BLOCK1_END)
    sq, rinv, mean = carve(1024), carve(512), carve(512)
    GI, SG, CA = carve(512), carve(512), carve(512)
    PA, PB = carve(NS, T + 2), carve(NS, T + TAPS_B - 1)
    Z = carve(JB, NS * T)
    Y = carve(KB, NS * T)
    act.after(m_x, m_ctx)
    dve.after(m_x, m_ctx)
    u_ready = modulated(0, 0, (0, 1), 5, sq, rinv)
    fill(PA, 0.0)
    m_pads = fill(PB, 0.0)
    pending = [(0, 1), (0, 2), (1, 0), (1, 1), (1, 2)]
    ada_done = {}
    w_in = a["w_in_ab"][0]
    GROUP = {"gate_out": 0, "gate_in": 1, "val": 2, "glu_a": 3, "glu_g": 4}
    both = lambda x: x.rearrange("p (s t) -> p s t", s=NS)

    def tap(name, k, j):
        return vec(name, k * JB + j)

    for jp in range(JB // 2):
        w = {g: fetch(columns_of(w_in, AW * GROUP[g] + 256 * jp)) for g in ("gate_in", "val", "glu_g", "glu_a", "gate_out")}
        for jj in range(2):
            j, got = 2 * jp + jj, {}
            for b, (g, (tile, there)) in enumerate(w.items()):
                pe.after(there)
                pe.after(bank_read[b])
                for k in range(KB):
                    pe.after(u_ready[k])
                    ins = mm(both(banks[b][:, :]), tile[:, k, P * jj:P * jj + P], U[:, :, k, :], k == 0, k == KB - 1)
                got[g] = (chunks_read if jj else pe.count).step(ins)
                if g == "gate_in":
                    m_gi = bank_read[b] = copy_a(GI, banks[b][:, :], got[g], dve.last())
                elif g == "val":
                    m_pa = bank_read[b] = VV(PA[:, :, 1:T + 1], both(banks[b][:, :]), both(GI), ALU.mult,
                                             marks=[got[g], m_gi, m_pads, dve.last()])
                elif g == "glu_g":
                    m_sg = bank_read[b] = A(SG, banks[b][:, :], ACT.Sigmoid, got[g], dve.last())
                elif g == "glu_a":
                    m_pb = bank_read[b] = VV(PB[:, :, 15:T + 15], both(banks[b][:, :]), both(SG), ALU.mult,
                                             marks=[got[g], m_sg])
            m = TS(both(CA), PA[:, :, 0:T], tap("conv_a", 0, j), ALU.mult, marks=[m_pa])
            for k in range(1, TAPS_A):
                m = STT(both(CA), PA[:, :, k:k + T], tap("conv_a", k, j), both(CA), ALU.mult, ALU.add, marks=[m])
            bank_read[4] = VV(Y[:, j, :], CA, banks[4][:, :], ALU.mult, marks=[m, got["gate_out"]])
            z_j = both(Z[:, j, :])
            m = TS(z_j, PB[:, :, 0:T], tap("conv_b", 0, j), ALU.mult, vec("conv_b_bias", j), ALU.add, marks=[m_pb])
            for k in range(1, TAPS_B):
                m = STT(z_j, PB[:, :, k:k + T], tap("conv_b", k, j), z_j, ALU.mult, ALU.add, marks=[m])
        for _ in range(2):
            l, pair = pending.pop(0)
            ada_done[l, pair] = ada(l, pair)
    m_z = m
    while pending:
        l, pair = pending.pop(0)
        ada_done[l, pair] = ada(l, pair)
    pe.after(m_z)
    pe.after(bank_read[0])
    for j in range(JB):
        ins = mm(banks[0][:, :], ones, Z[:, j, :], j == 0, j == JB - 1)
    m_mean = bank_read[0] = TS(mean, banks[0][:, :], 1.0 / AW, ALU.mult, marks=[pe.done(ins)])
    read = [None, None]
    pe.after(bank_read[1])
    for j in range(JB):
        m = VV(Z[:, j, :], Z[:, j, :], mean, ALU.subtract, marks=[m_mean])
        pe.after(A(sq[:, 512 * (j % 2):512 * (j % 2) + 512], Z[:, j, :], ACT.Square, m, read[j % 2]))
        read[j % 2] = pe.done(mm(banks[1][:, :], ones, sq[:, 512 * (j % 2):512 * (j % 2) + 512], j == 0, j == JB - 1))
    bank_read[1], m = inverse_rms(rinv, banks[1][:, :], 1.0 / AW, EPS, read[1])
    for j in range(JB):
        v = VV(Z[:, j, :], Z[:, j, :], rinv, ALU.mult, marks=[m])
        m_y = A(Y[:, JB + j, :], Z[:, j, :], ACT.Silu, v, bias=vec("ln_b_b", j), scale=vec("ln_b_g", j))

    def project_back(w, rhs, l, streams, m):
        pe.after(m)
        for c in range(KB // 2):
            tile, there = fetch(columns_of(w, 256 * c))
            pe.after(there)
            for half in range(2):
                n, b = 2 * c + half, 2 + (2 * c + half) % 4
                pe.after(bank_read[b])
                w_ = len(streams) * T
                for k in range(KB):
                    ins = mm(banks[b][:, 0:w_], tile[:, k, P * half:P * half + P], rhs[:, k, :], k == 0, k == KB - 1)
                m = (chunks_read if half else pe.count).step(ins)
                for i, s in enumerate(streams):
                    bank_read[b] = STT(H[:, s, n, :], banks[b][:, i * T:i * T + T], MOD[:, l, 2, n, s:s + 1],
                                       H[:, s, n, :], ALU.mult, ALU.add, marks=[m])

    for (l, n), pair in {(0, 1): 2, (1, 0): 0, (1, 1): 2}.items():
        fold(l, n, ada_done[l, pair])
    project_back(a["w_out_ab"][0], Y, 0, (0, 1), m_y)

    def moe(l, streams):
        S = len(streams)
        lo = streams[0]
        assert 3 * D * D == SLOTS * P * SLOT
        weights = [a["w_gate"], a["w_up"], a["w_down"]]

        def chunk(g, e, which, r):
            w, there = fetch(weights[which][l, g * EG + e, 2 * P * r:2 * P * (r + 1), :])
            pe.after(there)
            return w

        meet()
        carve = Carve(0, BLOCK1_END)
        U2T = carve(2 * S, D)
        OH = carve(2 * S, NE * CAP)
        OHW = carve(2 * S, NE * CAP)
        SW = carve(NE // EG, S * T)
        SG, HH, HT = carve(512), carve(512), carve(4, 2 * CAP * 2)
        AF, POS, tmp = carve(TT, S * NE), carve(TT, S * NE), carve(TT * S, NE)
        W0, W1, mask, cum = carve(T), carve(T), carve(T), carve(T)
        m8, ones_row = carve(8), carve(T)
        mx, sm = carve(TT * S), carve(TT * S)
        YG = OHW[:, 0:2 * S, :].rearrange("p (s h) n -> p s (h n)", s=S)
        sq = Carve(0, 1024, U2T.rearrange("p a b -> p (a b)")[:, 0:1024])(1024)
        rinv = HT.rearrange("p a b -> p (a b)")
        u_ready = modulated(l, 1, streams, 7, sq, rinv)
        fill(ones_row, 1.0)
        pe.after(bank_read[0])
        for t in range(TT):
            for i, s in enumerate(streams):
                c = (t * S + i) * NE
                for k in range(KB):
                    pe.after(u_ready[k])
                    ins = mm(banks[0][:, c:c + NE], U[:, s, k, P * t:P * t + P],
                             vec("w_router", (l * KB + k) * NE, NE), k == 0, k == KB - 1)
        m = pe.done(ins)
        for i, s in enumerate(streams):
            for t in range(TT):
                for half in range(2):
                    b = 1 + (2 * t + half) % 4
                    pe.after(bank_read[b])
                    for c in range(4):
                        ins = turn_over(banks[b][:, P * c:P * c + P], U[:, s, 4 * half + c, P * t:P * t + P])
                    m_turn = bank_read[b] = copy_a(U2T[:, 2 * i + t, 512 * half:512 * half + 512], banks[b][:, :],
                                                   pe.done(ins), u_ready[-1])
        logits = banks[0][:, 0:TT * S * NE].rearrange("p (a e) -> p a e", e=NE)
        af = AF.rearrange("p t (s e) -> p (t s) e", e=NE)
        wide = lambda x: x.rearrange("p (a o) -> p a o", o=1).broadcast_to([P, TT * S, NE])
        m = RED(mx, logits, ALU.max, marks=[m])
        m = bank_read[0] = VV(tmp, logits, wide(mx), ALU.subtract, marks=[m])
        m = A(tmp, tmp, ACT.Exp, m)
        m = RED(sm, tmp, ALU.add, marks=[m])
        m = RECIP(sm, sm, m)
        m_af = VV(af, tmp, wide(sm), ALU.mult, marks=[m])
        R = S * NE
        pe.after(bank_read[5])
        for t in range(TT):
            ins = turn_over(banks[5][0:R, P * t:P * t + P], AF[:, t, :], m_af)
        m = bank_read[5] = copy_v(W0[0:R, :], banks[5][0:R, 0:T], pe.done(ins))
        src, dst = W0, W1
        for _ in range(CAP // 8):
            dve.after(m)
            m = dve.done(nc.vector.max(m8[0:R, :], src[0:R, :]))
            dve.after(m)
            m = dve.done(nc.vector.match_replace(dst[0:R, :], m8[0:R, :], src[0:R, :], -1.0))
            src, dst = dst, src
        m = TS(mask[0:R, :], src[0:R, :], 0.0, ALU.is_lt, marks=[m])
        dve.after(m)
        m = dve.done(nc.vector.tensor_tensor_scan(cum[0:R, :], ones_row[0:R, :], mask[0:R, :], 0.0, ALU.mult, ALU.add))
        m = VV(cum[0:R, :], cum[0:R, :], mask[0:R, :], ALU.mult, marks=[m])
        m = TS(cum[0:R, :], cum[0:R, :], -1.0, ALU.add, marks=[m])
        pe.after(bank_read[6])
        for t in range(TT):
            ins = turn_over(banks[6][:, R * t:R * t + R], cum[0:R, P * t:P * t + P], m)
        m = bank_read[6] = copy_v(POS.rearrange("p t r -> p (t r)"), banks[6][:, 0:TT * R], pe.done(ins))
        slot_no = kept("slot_no").rearrange("p (o j) -> p o j", o=1).broadcast_to([P, NE, CAP])
        for i in range(S):
            for t in range(TT):
                at = lambda x: x[:, t, NE * i:NE * i + NE].rearrange("p (e o) -> p e o", o=1).broadcast_to([P, NE, CAP])
                hot = lambda x: x[:, 2 * i + t, :].rearrange("p (e j) -> p e j", j=CAP)
                m_oh = VV(hot(OH), slot_no, at(POS), ALU.is_equal, marks=[m])
                m_ohw = VV(hot(OHW), hot(OH), at(AF), ALU.mult, marks=[m_oh])
        for g in range(NE // EG):
            b = 1 + g
            pe.after(bank_read[b])
            for i in range(S):
                for t in range(TT):
                    ins = turn_over(banks[b][:, (2 * i + t) * P:(2 * i + t + 1) * P], OHW[:, 2 * i + t, P * g:P * g + P], m_ohw)
            bank_read[b] = copy_a(SW[:, g, :], banks[b][:, 0:S * T], pe.done(ins))
        GATE, UP, TURN, DOWN, OUT = 0, 1, 3, 4, 5
        XE = U[:, 0].rearrange("p k (e m) -> p k e m", e=EG)
        fill(XE, 0.0, m_turn)
        swf = SW.rearrange("p g n -> p (g n)")
        with turns_of(nc, f"experts{l}", NE // EG, [*workers, sp],
                      [*(q.count for q in workers), chunks_read, *landed], known, made) as (loop, g):
            meet()
            m_xe = []
            for q, b in enumerate((2, 5, 6, 7)):
                for k in (2 * q, 2 * q + 1):
                    for i in range(S):
                        c = S * P * (k % 2) + P * i
                        for t in range(TT):
                            ins = mm(banks[b][:, c:c + P], U2T[:, 2 * i + t, P * k:P * k + P],
                                     OH[:, 2 * i + t, bass.ds(g * P, P)], t == 0, t == TT - 1)
                m = pe.done(ins)
                for k in (2 * q, 2 * q + 1):
                    got = banks[b][:, S * P * (k % 2):S * P * (k % 2) + S * P].rearrange("p (i e j) -> p i e j", i=S, e=EG)
                    to = XE[:, k].rearrange("p e (i j) -> p i e j", i=NS)[:, 0:S]
                    m_xe.append((copy_v if q % 2 else copy_a)(to, got, m))
            read = {b: m_xe for b in range(8)}

            for e in range(EG):
                for which, b in ((0, GATE), (1, UP)):
                    if e > 0:
                        pe.after(read[b])
                    for r in range(KB // 2):
                        w = chunk(g, e, which, r)
                        for kk in range(2):
                            k = 2 * r + kk
                            pe.after(m_xe[k])
                            for half in range(2):
                                ins = mm(banks[b][64 * half:64 * half + 64, :], XE[:, k, e, :],
                                         w[:, kk, 512 * half:512 * half + 512], k == 0, k == KB - 1)
                        m = chunks_read.step(ins)
                    if which == 0:
                        m_sg = read[b] = A(SG, banks[b][:, :], ACT.Silu, m, dve.last())
                    else:
                        m_hh = read[b] = VV(HH, banks[b][:, :], SG, ALU.mult, marks=[m, m_sg])
                pe.after(read[TURN])
                for c in range(4):
                    ins = turn_over(banks[TURN][:, P * c:P * c + P], HH[:, P * c:P * c + P], m_hh)
                m_ht = read[TURN] = copy_v(HT.rearrange("p a b -> p (a b)"), banks[TURN][:, :], pe.done(ins))
                pe.after(m_ht, read[DOWN])
                for r in range(KB // 2):
                    w = chunk(g, e, 2, r)
                    for kk in range(2):
                        k = 2 * r + kk
                        half, c = divmod(k, 4)
                        for out_half in range(2):
                            ins = mm(banks[DOWN][64 * out_half:64 * out_half + 64, :], HT[:, c, 64 * half:64 * half + 64],
                                     w[:, kk, 512 * out_half:512 * out_half + 512], k == 0, k == KB - 1)
                    m = chunks_read.step(ins)
                for i in range(S):
                    for out_half, copy in ((0, copy_a), (1, copy_v)):
                        p0 = 64 * out_half + CAP * i
                        m_c = copy(YG[CAP * e:CAP * e + CAP, i, 512 * out_half:512 * out_half + 512],
                                   banks[DOWN][p0:p0 + CAP, :], m)
                read[DOWN] = (act.last(), dve.last())
            pe.after(act.last(), dve.last())
            for n in range(KB):
                b = OUT + n % 3
                if n >= 3:
                    pe.after(read[b])
                for i in range(S):
                    ins = mm(banks[b][:, T * i:T * i + T], YG[:, i, P * n:P * n + P],
                             swf[:, bass.ds(g * (S * T) + T * i, T)], True, True)
                m = pe.done(ins)
                for i, s in enumerate(streams):
                    read[b] = STT(H[:, s, n, :], banks[b][:, T * i:T * i + T], MOD[:, l, 5, n, s:s + 1], H[:, s, n, :],
                                  ALU.mult, ALU.add, marks=[m])
        issued[0] = chunks_read.n
        for b in range(8):
            bank_read[b] = [act.last(), dve.last()]

    moe(0, (0, 1))

    meet()
    carve = Carve(0, BLOCK1_END)
    Q, K = carve(HEADS, T), carve(HEADS, NS * T)
    V = carve(NS * TT, HEADS * P)
    at_var = carve.at
    var = carve(3072)
    reuse = Carve(at_var, at_var + 3072)
    Y, PT = reuse(KB, T), reuse(2 * TT, TT * P)
    PROD, GO = carve(JB, T), carve(JB, T)
    UT = carve(TT, AW)
    sq = carve(1024)
    rinv = carve(512)
    pad = carve(2, T + 2)
    t1, t2 = sq[:, 0:512], sq[:, 512:1024]
    r0, lam, gq8, gsub = carve(16), carve(4), carve(1), carve(1)
    u_ready = modulated(1, 0, (0, 1), 7, sq, rinv)
    ctx_u = U[:, 1].rearrange("p k t -> p (k t)")
    ctx_h = H[:, 1].rearrange("p k t -> p (k t)")
    E = ctx_u.rearrange("p (b n) -> p b n", b=4)
    UF = ctx_h.rearrange("p (b n) -> p b n", b=4)
    w_in = a["w_in_cd"][0]
    m = VV(lam[:, 0:2], vec("lam_q1", 0, 2), vec("lam_k1", 0, 2), ALU.mult)
    m_gq = TS(gq8, vec("g_q"), DH ** -0.5, ALU.mult)
    m_gsub = TS(gsub, vec("g_subln"), 1.0 - LAM_INIT, ALU.mult)
    pe.after(bank_read[6])
    pe.after(m)
    m = pe.done(mm(banks[6][:, 0:2], ones, lam[:, 0:2], True, True))
    m = bank_read[6] = A(lam[:, 2:4], banks[6][:, 0:2], ACT.Exp, m)
    m_lam = STT(lam[:, 0:1], lam[:, 2:3], LAM_INIT, lam[:, 3:4], ALU.add, ALU.subtract, marks=[m])

    def squares(flat, b, b2, out, n, m):
        m_sq = A(flat, banks[b][:, 0:n], ACT.Square, m, pe.last())
        bank_read[b] = m_sq
        pe.after(bank_read[b2])
        pe.after(m_sq)
        m = pe.done(mm(banks[b2][:, 0:n], halves, flat, True, True))
        bank_read[b2] = TS(out, banks[b2][:, 0:n], 1.0 / DH, ALU.mult, EPS, ALU.add, marks=[m])
        return bank_read[b2]

    def project_heads(c0, dst, var_at, rhs, n, turn):
        later = None
        for c in range(2):
            tile, there = fetch(columns_of(w_in, c0 + 256 * c))
            pe.after(there)
            for half in range(2):
                h = 2 * c + half
                b = (turn + h) % 4
                pe.after(bank_read[b])
                for k in range(KB):
                    pe.after(u_ready[k])
                    ins = mm(banks[b][:, 0:n], tile[:, k, P * half:P * half + P], rhs(k), k == 0, k == KB - 1)
                m = (chunks_read if half else pe.count).step(ins)
                if later:
                    later()
                m_c = copy_a(dst[:, h, :], banks[b][:, 0:n], m)
                later = (lambda b=b, h=h, m_c=m_c: squares(sq[:, 512 * (h % 2):512 * (h % 2) + n], b, 4 + h % 2,
                                                           var[:, var_at + h * n:var_at + h * n + n], n, m_c))
                bank_read[b] = m_c
        return later

    last_k = project_heads(512, K, 1024, lambda k: U[:, :, k, :], 512, 0)
    tiles = [fetch(columns_of(w_in, 1024 + 256 * c)) for c in range(2)]
    for s in range(NS):
        for t in range(TT):
            b = 6 + t
            pe.after(bank_read[b])
            for c, (tile, there) in enumerate(tiles):
                pe.after(there)
                for k in range(KB):
                    ins = mm(banks[b][:, 256 * c:256 * c + 256], U[:, s, k, P * t:P * t + P], tile[:, k, :],
                             k == 0, k == KB - 1)
            m_v = chunks_read.step(ins, 2) if (s, t) == (NS - 1, TT - 1) else pe.done(ins)
            bank_read[b] = copy_v(V[:, 2 * s + t, :], banks[b][:, :], m_v)
            if last_k:
                last_k()
                last_k = None
    m_vcopy = bank_read[7]
    last_q = project_heads(0, Q, 0, lambda k: U[:, 0, k, :], T, 0)

    def short_conv(c):
        for n, (first, dst) in enumerate(((512, PROD), (1024, None), (0, GO))):
            tile, there = fetch(columns_of(w_in, 1536 + first + 256 * c))
            b = 6 + n % 2
            pe.after(there)
            pe.after(bank_read[b])
            for half in range(2):
                for k in range(KB):
                    ins = mm(banks[b][:, T * half:T * half + T], tile[:, k, P * half:P * half + P], U[:, 0, k, :],
                             k == 0, k == KB - 1)
            m = chunks_read.step(ins)
            m = bank_read[b] = copy_a(pad[:, :, 1:T + 1], banks[b][:, :].rearrange("p (c t) -> p c t", c=2), m, dve.last())
            for half in range(2):
                blk = first // P + 2 * c + half
                o = rinv[:, T * half:T * half + T] if dst is None else dst[:, 2 * c + half, :]
                m2 = TS(o, pad[:, half, 0:T], vec("conv_d", blk), ALU.mult, marks=[m])
                for k in range(1, 3):
                    m2 = STT(o, pad[:, half, k:k + T], vec("conv_d", k * 3 * JB + blk), o, ALU.mult, ALU.add, marks=[m2])
                if dst is None:
                    m2 = VV(PROD[:, 2 * c + half, :], PROD[:, 2 * c + half, :], o, ALU.mult, marks=[m2])
        return m2

    fill(pad, 0.0, act.last())
    m_pad = dve.last()
    act.after(m_pad)
    last_q()
    m_var = dve.last()
    short_conv(0)
    m = RECIP(var, var, m_var)
    m_var = A(var, var, ACT.Sqrt, m)

    def rope(x, b, tmp, m):
        pe.after(bank_read[b])
        pe.after(m)
        m = pe.done(mm(banks[b][:, 0:T], kept("rope_swap"), x, True, True))
        m = bank_read[b] = VV(tmp, banks[b][:, 0:T], SIN, ALU.mult, marks=[m, m_middle])
        m2 = VV(x, x, COS, ALU.mult, marks=[pe.last()])
        return VV(x, x, tmp, ALU.add, marks=[m, m2])

    normed = []
    for h in range(HEADS):
        n = STT(K[:, h, :], K[:, h, :], vec("g_k"), var[:, 1024 + 512 * h:1536 + 512 * h], ALU.mult, ALU.mult, marks=[m_var])
        normed.append((K[:, h, 0:T], n))
        n = STT(Q[:, h, :], Q[:, h, :], gq8, var[:, T * h:T * h + T], ALU.mult, ALU.mult, marks=[m_var, m_gq])
        normed.append((Q[:, h, :], n))
    for n, (x, m) in enumerate(normed):
        m_roped = rope(x, n % 4, sq[:, 512 + T * (n % 2):512 + T * (n % 2) + T], m)

    def scores(h):
        pe.after(m_roped)
        for qt in range(TT):
            for j in range(2):
                pe.after(bank_read[2 * qt + j])
                ins = mm(banks[2 * qt + j][:, :], Q[64 * j:64 * j + 64, h, P * qt:P * qt + P],
                         K[64 * j:64 * j + 64, h, :], True, True)
            got = pe.done(ins)
            for j in range(2):
                b = 2 * qt + j
                stat = r0[:, 4 * b:4 * b + 4]
                m = RED(stat[:, 0:1], banks[b][:, :], ALU.max, marks=[got, dve.last(), act.last()], negate=True)
                m = bank_read[b] = A(E[:, b, :], banks[b][:, :], ACT.Exp, m, pe.last(), dve.last(), bias=stat[:, 0:1],
                                     accum=stat[:, 1:2])
                RECIP(stat[:, 2:3], stat[:, 1:2], m)
            s0, s1 = r0[:, 8 * qt:8 * qt + 4], r0[:, 8 * qt + 4:8 * qt + 8]
            m = VV(s1[:, 3:4], s1[:, 2:3], lam[:, 0:1], ALU.mult, marks=[dve.last(), m_lam])
            m = TS(E[:, 2 * qt + 1, :], E[:, 2 * qt + 1, :], s1[:, 3:4], ALU.mult, marks=[m])
            m = STT(E[:, 2 * qt, :], E[:, 2 * qt, :], s0[:, 2:3], E[:, 2 * qt + 1, :], ALU.mult, ALU.subtract, marks=[m])
        return m

    def values(h, m):
        for qt in range(TT):
            pe.after(bank_read[4])
            for kb in range(4):
                ins = turn_over(banks[4][:, P * kb:P * kb + P], E[:, 2 * qt, P * kb:P * kb + P], m)
            m_t = bank_read[4] = copy_a(PT[:, :, P * qt:P * qt + P], banks[4][:, :].rearrange("p (k q) -> p k q", k=4),
                                        pe.done(ins), m_var)
        pe.after(bank_read[5])
        pe.after(m_t, m_vcopy)
        for kb in range(4):
            ins = mm(banks[5][:, 0:T], V[:, kb, P * h:P * h + P], PT[:, kb, :], kb == 0, kb == 3)
        got = pe.done(ins)
        m = A(Y[:, h, :], banks[5][:, 0:T], ACT.Square, got)
        pe.after(m)
        m = pe.done(mm(banks[5][:, T:2 * T], ones, Y[:, h, :], True, True))
        _, m = inverse_rms(Y[:, h, :], banks[5][:, T:2 * T], 1.0 / P, SUB_EPS, m)
        bank_read[5] = STT(Y[:, h, :], banks[5][:, 0:T], gsub, Y[:, h, :], ALU.mult, ALU.mult, marks=[m, m_gsub])

    def spectrum(m):
        for t in range(TT):
            b = 6 + t
            pe.after(bank_read[b])
            for blk in range(JB):
                ins = turn_over(banks[b][:, P * blk:P * blk + P], PROD[:, blk, P * t:P * t + P], m)
            m2 = bank_read[b] = copy_a(UT[:, t, :], banks[b][:, :], pe.done(ins))
        pe.after(m2)
        for f in range(4):
            b = 6 + f % 2
            pe.after(bank_read[b])
            for t in range(TT):
                ins = mm(banks[b][:, :], dft[:, t, P * f:P * f + P], UT[:, t, :], t == 0, t == TT - 1)
            m = bank_read[b] = copy_v(UF[:, f, :], banks[b][:, :], pe.done(ins))
        for f in range(2):
            re, im, hre, him = UF[:, f, :], UF[:, 2 + f, :], HF[:, f, :], HF[:, 2 + f, :]
            m1 = VV(t1, re, hre, ALU.mult, marks=[m])
            m2 = VV(t2, im, him, ALU.mult)
            m3 = VV(him, re, him, ALU.mult, marks=[m2])
            m4 = VV(hre, im, hre, ALU.mult, marks=[m1])
            VV(re, t1, t2, ALU.subtract, marks=[m4])
            m = VV(im, him, hre, ALU.add, marks=[m4])
        return m

    def back_in_time(m):
        pe.after(m, m_middle)
        for blk in range(JB):
            b = 6 + blk % 2
            pe.after(bank_read[b])
            for f in range(4):
                ins = mm(banks[b][:, 0:T], UF[:, f, P * blk:P * blk + P], idft[:, f, :], f == 0, f == 3)
            m = bank_read[b] = STT(Y[:, HEADS + blk, :], PROD[:, blk, :], vec("hf_bias", blk), banks[b][:, 0:T],
                                   ALU.mult, ALU.add, marks=[pe.done(ins)])
            m = VV(Y[:, HEADS + blk, :], Y[:, HEADS + blk, :], GO[:, blk, :], ALU.mult, marks=[m])
        return m

    p0 = scores(0)
    m_prod = short_conv(1)
    values(0, p0)
    p1 = scores(1)
    m_freq = spectrum(m_prod)
    values(1, p1)
    p2 = scores(2)
    m_hy = back_in_time(m_freq)
    values(2, p2)
    p3 = scores(3)
    values(3, p3)
    project_back(a["w_out_cd"][0], Y, 1, (0,), [m_hy, dve.last()])
    meet()
    carve = Carve()
    NA_BIAS = carve(NA_H, TT, T)
    GATES = carve(2 * KB, T)
    HID = carve(FB, T)
    assert BLOCK1_END <= carve.at
    NA_MASK = carve(TT, T)
    SW_BIAS = carve(SW_H, TT, T)
    by_the_way = Carve(0, KB * T, ctx_u)
    sw_mask, hot, table, dist = by_the_way(TT, T), by_the_way(2 * T), by_the_way(SW_H), by_the_way(2 * T)
    in_late, out_dist, in_bias = counted("in_late"), counted("out_distance"), counted("in_sw_bias")
    late = [load(in_late, NA_MASK.rearrange("p t k -> p (t k)"), a["late"][:, 0:512], pool),
            load(in_late, sw_mask.rearrange("p t k -> p (t k)"), a["late"][:, 512:1024], pool),
            load(in_late, hot, a["late"][:, 1024:1536], pool),
            load(in_late, table[0:32, :], a["t5_rel_table_2"], pool)][-1]
    pe.after(bank_read[0])
    pe.after(late)
    m = pe.done(mm(banks[0][0:SW_H, :], table[0:32, :], hot[0:32, :], True, True))
    m = bank_read[0] = copy_v(dist[0:SW_H, :], banks[0][0:SW_H, :], m)
    scratch = nc.dram_tensor("distance_bias", (SW_H, 2 * T), F32, kind="Internal").ap()
    m = load(out_dist, scratch, dist[0:SW_H, :], pool, [m])
    for t in range(TT):
        pairs = bass.AP(tensor=scratch.tensor, offset=P - P * t, ap=[[1, P], [2 * T, SW_H], [1, T]])
        m_pairs = load(in_bias, SW_BIAS[:, :, t, :], pairs, pool, [m])
    for t in range(TT):
        m_sw_bias = VV(SW_BIAS[:, :, t, :], SW_BIAS[:, :, t, :],
                       sw_mask[:, t, :].rearrange("p (o k) -> p o k", o=1).broadcast_to([P, SW_H, T]), ALU.add,
                       marks=[m_pairs, late])

    moe(1, (0,))

    meet()
    h0 = H[:, 0]
    spare = H[:, 1].rearrange("p k t -> p (k t)")
    OUT2 = U[:, 1]
    merged = H[:, 1]
    free_g = Carve(0, 2 * KB * T, GATES.rearrange("p n t -> p (n t)"))
    var, rinv = free_g(13, T), free_g(T)
    sg = [GATES.rearrange("p n t -> p (n t)")[:, 512 * n:512 * n + 512] for n in range(2)]
    heads = Carve(0, FB * T, HID.rearrange("p n t -> p (n t)"))
    QA, KA, QS, KS, KSX = heads(4, T), heads(4, T), heads(4, T), heads(T), heads(T)
    VA, VS = heads(TT, 512), heads(TT, P)
    sq = spare[:, 0:1024]
    SC = [spare[:, 512 * n:512 * n + 512].rearrange("p (t k) -> p t k", t=TT) for n in range(2)]
    PT = [spare[:, 1024 + 512 * n:1536 + 512 * n].rearrange("p (k q) -> p k q", k=TT) for n in range(2)]
    g8 = small[:, 0:2]
    stats = small[:, 16:16 + 16 * 8]
    in_bias_na = counted("in_na_bias")

    def now(name, i=0):
        c = LVEC[name][0] + i
        return cur[:, c:c + 1]

    def load_na_bias(l):
        for r in range(ROWS):
            for kr in range(ROWS):
                src = bass.AP(tensor=a["na_rpb_2"].tensor, ap=[[1, GRID], [RPB_R * RPB_C, NA_H], [1, GRID]],
                              offset=l * (NA_H * RPB_R * RPB_C) + (kr - r + 7) * RPB_C + 15 - (GRID - 1))
                p0 = GRID * (1 - r % 2)
                m = load(in_bias_na, NA_BIAS[p0:p0 + GRID, :, r // 2, GRID * kr:GRID * kr + GRID], src)
        return m

    def reversed_queries(x):
        return x.rearrange("p (n q) -> p n q", q=P)[:, :, ::-1]

    with turns_of(nc, "layers", LAYERS, [*workers, sp],
                  [*(q.count for q in workers), chunks_read, *landed, in_bias_na], known, made) as (loop, l):
        meet()
        first = issued[0]
        read = {b: None for b in range(8)}

        def chunk(w, rows, cols):
            tile, there = fetch(w[l, rows, cols])
            pe.after(there)
            return tile

        def wide(w, c):
            return chunk(w, slice(0, D), slice(256 * c, 256 * c + 256))

        m = copy_v(cur[:, :], lvec_mem[:, bass.ds(l * NLVEC, NLVEC)], m_layers)
        m_sink = copy_v(small[:, 2:2 + SW_H], sink_mem[:, bass.ds(l * SW_H, SW_H)])
        m = TS(g8[:, 0:1], now("na_q_norm"), DH ** -0.5, ALU.mult, marks=[m])
        m_g8 = TS(g8[:, 1:2], now("sw_q_norm"), DH ** -0.5, ALU.mult)
        def normed(name, b):
            rd = [None, None]
            pe.after(read[b])
            for k in range(KB):
                part = sq[:, 512 * (k % 2):512 * (k % 2) + T]
                pe.after(A(part, h0[:, k, :], ACT.Square, rd[k % 2], dve.last()))
                rd[k % 2] = pe.done(mm(banks[b][:, 0:T], ones, part, k == 0, k == KB - 1))
            read[b], m = inverse_rms(rinv, banks[b][:, 0:T], 1.0 / D, EPS, rd[1])
            return [STT(U[:, 0, k, :], h0[:, k, :], now(name, k), rinv, ALU.mult, ALU.mult, marks=[m])
                    for k in range(KB)]

        def project(tile, b, ready, halves_=2):
            pe.after(read[b])
            for half in range(halves_):
                for k in range(KB):
                    pe.after(ready[k])
                    ins = mm(banks[b][:, T * half:T * half + T], tile[:, k, P * half:P * half + P], U[:, 0, k, :],
                             k == 0, k == KB - 1)
            return (chunks_read if halves_ == 2 else pe.count).step(ins)

        def ffn(n, idle=0):
            gate, up, down = (a[f"ffn{n}_w_{x}_2"] for x in ("gate", "up", "down"))
            ready = normed(f"ffn{n}_norm", 7)
            for c in range(FB // 2):
                b = c % 2
                m = project(wide(gate, c), b, ready)
                m_s = read[b] = A(sg[c % 2], banks[b][:, :], ACT.Silu, m, dve.last())
                m = project(wide(up, c), 2 + b, ready)
                m_h = read[2 + b] = VV(HID[:, 2 * c:2 * c + 2, :].rearrange("p n t -> p (n t)"), banks[2 + b][:, :],
                                       sg[c % 2], ALU.mult, marks=[m, m_s])
            pe.after(*(read[b] for b in range(4, 8)))
            for c in range(FB // 2):
                w = chunk(down, slice(256 * c, 256 * c + 256), slice(0, D))
                pe.after(m_h)
                for kk in range(2):
                    k = 2 * c + kk
                    for n in range(KB):
                        ins = mm(banks[4 + n // 2][:, T * (n % 2):T * (n % 2) + T], w[:, kk, P * n:P * n + P],
                                 HID[:, k, :], k == 0 and n % 2 == 0, k == FB - 1)
                m = chunks_read.step(ins, 1 + (idle if c == FB // 2 - 1 else 0))
            for p in range(KB // 2):
                read[4 + p] = STT(h0[:, 2 * p:2 * p + 2, :], banks[4 + p][:, :].rearrange("p (n t) -> p n t", n=2), 0.5,
                                  h0[:, 2 * p:2 * p + 2, :], ALU.mult, ALU.add, marks=[m])

        ffn(1)
        m_rpb = load_na_bias(l)
        for t in range(TT):
            pool.after(m_rpb, late)
            m_na_bias = pool.done(nc.gpsimd.tensor_tensor(
                NA_BIAS[:, :, t, :], NA_BIAS[:, :, t, :],
                NA_MASK[:, t, :].rearrange("p (o k) -> p o k", o=1).broadcast_to([P, NA_H, T]), ALU.add))
        meet()

        ready = normed("mix_norm", 7)
        n_var, later, m_v2 = 0, None, None

        def head_squares(b, n, v, m, slot, queries=False):
            w = T * n
            to, got = sq[:, 512 * slot:512 * slot + w], banks[b][:, 0:w]
            if queries:
                to, got = reversed_queries(to), got.rearrange("p (n q) -> p n q", q=P)
            m = read[b] = A(to, got, ACT.Square, m, pe.last())
            pe.after(m, read[6])
            m = pe.done(mm(banks[6][:, 0:w], halves, sq[:, 512 * slot:512 * slot + w], True, True))
            read[6] = TS(var[:, v:v + n, :].rearrange("p n t -> p (n t)"), banks[6][:, 0:w], 1.0 / DH, ALU.mult,
                         EPS, ALU.add, marks=[m])
            return read[6]

        flip = [0]

        def next_bank():
            flip[0] ^= 1
            return 4 + flip[0]

        w_in = a["w_in_2"]

        def heads_in(dst, v, first_chunk, queries=False):
            nonlocal later
            for c in range(2):
                b = next_bank()
                m = project(wide(w_in, first_chunk + c), b, ready)
                if later:
                    later()
                to, got = dst[:, 2 * c:2 * c + 2, :].rearrange("p n t -> p (n t)"), banks[b][:, :]
                if queries:
                    to, got = reversed_queries(to), got.rearrange("p (n q) -> p n q", q=P)
                m = read[b] = copy_v(to, got, m)
                later = lambda b=b, c=c, m=m: head_squares(b, 2, v + 2 * c, m, flip[0], queries)

        heads_in(QA, 0, 0, True)
        heads_in(KA, 4, 2)
        tiles = [wide(w_in, 4), wide(w_in, 5)]
        for t in range(TT):
            b = next_bank()
            pe.after(read[b])
            for c in range(2):
                for k in range(KB):
                    ins = mm(banks[b][:, 256 * c:256 * c + 256], U[:, 0, k, P * t:P * t + P], tiles[c][:, k, :],
                             k == 0, k == KB - 1)
            m = chunks_read.step(ins, 2) if t == TT - 1 else pe.done(ins)
            if later:
                later()
                later = None
            m_va = read[b] = copy_v(VA[:, t, :], banks[b][:, :], m)
        heads_in(QS, 8, 6, True)
        tile = wide(w_in, 8)
        b = next_bank()
        m = project(tile, b, ready, 1)
        later()
        m = copy_v(KS, banks[b][:, 0:T], m)
        m_var = head_squares(b, 1, 12, m, flip[0])
        b = next_bank()
        pe.after(read[b])
        for t in range(TT):
            for k in range(KB):
                ins = mm(banks[b][:, P * t:P * t + P], U[:, 0, k, P * t:P * t + P], tile[:, k, P:2 * P], k == 0, k == KB - 1)
        m = chunks_read.step(ins)
        m_vs = read[b] = copy_v(VS.rearrange("p t n -> p (t n)"), banks[b][:, 0:T], m)

        def gates(c):
            b = next_bank()
            m = project(wide(w_in, 9 + c), b, ready)
            for half in range(2):
                n = 2 * c + half
                read[b] = A(GATES[:, n, :], banks[b][:, T * half:T * half + T], ACT.Sigmoid, m, m_normed,
                            bias=now("b_gate", n))
            return read[b]

        flat = var.rearrange("p n t -> p (n t)")
        m = RECIP(flat, flat, m_var)
        m = A(flat, flat, ACT.Sqrt, m)
        for dst, g, v in ((QA, g8[:, 0:1], 0), (KA, now("na_k_norm"), 4), (QS, g8[:, 1:2], 8)):
            m_normed = STT(dst, dst, g, var[:, v:v + 4, :], ALU.mult, ALU.mult, marks=[m, m_g8])
        m_ks = STT(KS, KS, now("sw_k_norm"), var[:, 12, :], ALU.mult, ALU.mult, marks=[m])
        m_normed = copy_v(KSX[0:DH, :], KS[DH:P, :], m_ks)
        m_normed = copy_v(KSX[DH:P, :], KS[0:DH, :], m_ks)

        NA, SW = 0, 1
        work = [(kind, h) for kind in (NA, SW) for h in range(NA_H)]
        probs_read = [None, None]

        def scores(n):
            kind, h = work[n]
            p0, blk, b, i = DH * (h % 2), h // 2, n % 2, n % 2
            q = (QS if kind else QA)[p0:p0 + DH, blk, :]
            if kind:
                k = (KS if (h // 4) == h % 2 else KSX)[p0:p0 + DH, :]
            else:
                k = KA[p0:p0 + DH, blk, :]
            pe.after(read[b], m_normed)
            for t in range(TT):
                ins = mm(banks[b][:, T * t:T * t + T], q[:, P * t:P * t + P], k, True, True)
            m = pe.done(ins)
            bias = (SW_BIAS if kind else NA_BIAS)[:, h]
            m = read[b] = VV(SC[i], banks[b][:, :].rearrange("p (t k) -> p t k", t=TT), bias, ALU.add,
                             marks=[m, m_na_bias, m_sw_bias, probs_read[i]])
            st = stats[:, 64 * i:64 * i + 64]
            top, total, extra = st[:, 0:2], st[:, 2:4], st[:, 4:6]
            m = RED(top, SC[i], ALU.max, marks=[m], negate=True)
            if kind:
                m = TS(top, top, -1.0, ALU.mult, small[:, 2 + h:3 + h], ALU.max, marks=[m, m_sink])
                m = TS(top, top, -1.0, ALU.mult, marks=[m])
                A(extra, top, ACT.Exp, m, bias=small[:, 2 + h:3 + h])
            for t in range(TT):
                m_e = A(SC[i][:, t, :], SC[i][:, t, :], ACT.Exp, m, bias=top[:, t:t + 1], accum=total[:, t:t + 1])
            if kind:
                m_e = VV(total, total, extra, ALU.add, marks=[m_e])
            m = RECIP(total, total, m_e)
            for t in range(TT):
                m2 = TS(SC[i][:, t, :], SC[i][:, t, :], total[:, t:t + 1], ALU.mult, marks=[m])
            return m2

        def values(n, m):
            kind, h = work[n]
            p0, blk, i = DH * (h % 2), h // 2, n % 2
            pe.after(read[2], m)
            for k in range(TT):
                for t in range(TT):
                    ins = turn_over(banks[2][:, T * k + P * t:T * k + P * t + P], SC[i][:, t, P * k:P * k + P])
            probs_read[i] = pe.done(ins)
            m = read[2] = copy_a(reversed_queries(PT[i].rearrange("p k q -> p (k q)")),
                                 banks[2][:, :].rearrange("p (n q) -> p n q", q=P), probs_read[i])
            pe.after(m, read[3], m_va, m_vs)
            for k in range(TT):
                v = VS[:, k, DH * (h // 4):DH * (h // 4) + DH] if kind else VA[:, k, DH * h:DH * h + DH]
                ins = mm(banks[3][p0:p0 + DH, 0:T], v, PT[i][:, k, :], k == 0, k == TT - 1)
            m = pe.done(ins)
            if h % 2:
                read[3] = copy_a(OUT2[:, 4 * kind + blk, :], banks[3][:, 0:T], m)
            return m

        waiting = None
        for n in range(len(work)):
            m = scores(n)
            if n % 2 == 0:
                gates(n // 2)
            if waiting:
                values(n - 1, waiting)
            waiting = m
        values(len(work) - 1, waiting)
        m_attn = act.last()

        tiles = [chunk(w, slice(0, 512), slice(512 * c, 512 * c + 512))
                 for w in (a["w_branch_na_2"], a["w_branch_sw_2"]) for c in range(2)]
        pe.after(m_attn)
        t1 = [KA[:, 0:2, :].rearrange("p n t -> p (n t)"), KA[:, 2:4, :].rearrange("p n t -> p (n t)")]
        merged_at = []
        for p in range(KB // 2):
            c, off = divmod(p, 2)
            got = []
            for branch in range(2):
                b = 2 * (p % 2) + branch
                pe.after(read[b])
                for half in range(2):
                    for k in range(4):
                        ins = mm(banks[b][:, T * half:T * half + T],
                                 tiles[2 * branch + c][:, k, 256 * off + P * half:256 * off + P * half + P],
                                 OUT2[:, 4 * branch + k, :], k == 0, k == 3)
                got.append(chunks_read.step(ins, 4) if (p, branch) == (KB // 2 - 1, 1) else pe.done(ins))
            for branch in range(2):
                b = 2 * (p % 2) + branch
                g = GATES[:, KB * branch + 2 * p:KB * branch + 2 * p + 2, :].rearrange("p n t -> p (n t)")
                m = read[b] = VV(t1[branch], banks[b][:, :], g, ALU.mult, marks=[got[branch], m_attn, dve.last()])
            m = VV(merged[:, 2 * p:2 * p + 2, :].rearrange("p n t -> p (n t)"), t1[0], t1[1], ALU.add, marks=[m])
        pe.after(m)
        for c in range(KB // 2):
            tile, b = wide(a["w_out_2"], c), c % 4
            pe.after(read[b])
            for half in range(2):
                for k in range(KB):
                    ins = mm(banks[b][:, T * half:T * half + T], tile[:, k, P * half:P * half + P], merged[:, k, :],
                             k == 0, k == KB - 1)
            m = chunks_read.step(ins)
            read[b] = VV(h0[:, 2 * c:2 * c + 2, :].rearrange("p n t -> p (n t)"),
                         h0[:, 2 * c:2 * c + 2, :].rearrange("p n t -> p (n t)"), banks[b][:, :], ALU.add, marks=[m])
        meet()
        idle = -(issued[0] + 3 * FB // 2 - first) % SLOTS
        ffn(2, idle)
        issued[0] += idle
    issued[0] = chunks_read.n

    sent = counted("sent")
    sp.after([q.last() for q in workers], m_layers)
    sent.step(nc.sync.dma_start(out.rearrange("(k p) t -> p k t", p=P), h0))
    sp.after(Mark(sent, sent.n))
    return made


_WEIGHTS = ["w_ada", "w_in_ab", "w_out_ab", "w_in_cd", "w_out_cd", "w_gate", "w_up", "w_down", "hf_w1", "hf_w2",
            "hf_w3", "sw_sink_2", "t5_rel_table_2", "na_rpb_2", "ffn1_w_gate_2", "ffn1_w_up_2", "ffn1_w_down_2",
            "w_in_2", "w_branch_na_2", "w_branch_sw_2", "w_out_2", "ffn2_w_gate_2", "ffn2_w_up_2", "ffn2_w_down_2"]


def lay_out(inputs):
    given = {n: np.asarray(v) for n, v in inputs.items()}
    out = {n: np.ascontiguousarray(given[n]) for n in _WEIGHTS}
    out["x_t"] = np.ascontiguousarray(given["x"][0].T)
    out["ctx_t"] = np.ascontiguousarray(given["ctx"][0].T)
    out["vectors"] = pack_vectors(given)
    out["layer_vectors"] = pack_layer_vectors(given)
    out["kept"], out["early"], out["middle"], out["late"] = (kept_constants(), early_constants(), middle_constants(),
                                                            late_constants())
    return out


def kernel(**inputs):
    from concourse import bacc
    from concourse.bass_utils import run_bass_kernel_spmd

    arrays = lay_out(inputs)

    def build(known):
        nc = bacc.Bacc("TRN2", target_bir_lowering=False, num_devices=1)
        args = {n: nc.dram_tensor(f"in_{n}", v.shape, mybir.dt.from_np(v.dtype), kind="ExternalInput").ap()
                for n, v in arrays.items()}
        out = nc.dram_tensor("out", (D, T), F32, kind="ExternalOutput").ap()
        return nc, program(nc, args, out, known)

    _, known = build({})
    nc, _ = build(known)
    r = run_bass_kernel_spmd(nc, [{f"in_{n}": v for n, v in arrays.items()}], core_ids=[0])
    return np.ascontiguousarray(r.results[0]["out"].T)[None]
```

```python
import math
from contextlib import contextmanager

import numpy as np

import concourse.bass as bass
from concourse import mybir

F32 = mybir.dt.float32
ACT = mybir.ActivationFunctionType
ALU = mybir.AluOpType
AX = mybir.AxisListType
ET = mybir.EngineType

P = 128
D = 1024
KB = D // P
T = 256
NS = 2
TT = T // P
AW = 512
JB = AW // P
HEADS = 4
NE, CAP = 16, 32
EG = 4
TAPS_A, TAPS_B = 3, 31
FF = 2816
FB = FF // P
GRID = 64
ROWS = T // GRID
NA_H, SW_H, DH = 8, 8, 64
RPB_R, RPB_C = 15, 31
EPS, SUB_EPS = 1e-6, 1e-5
LAM_INIT = 0.8 - 0.6 * math.exp(-0.3)
NEG = -1e30
TWO_PI = 2.0 * math.pi
ROUND = 1.5 * 2.0 ** 23
SLOTS, SLOT = 12, 2048
ARENA = 18432
LAYERS = 2


def columns(*names):
    at, out = 0, {}
    for name, n in names:
        out[name] = (at, n)
        at += n
    return out, at


VEC, NVEC = columns(("c", KB), ("c_ctx", KB), ("b_ada", 2 * 6 * KB), ("g_mix", 2 * KB), ("g_ffn", 2 * KB),
                    ("conv_a", TAPS_A * JB), ("conv_b", TAPS_B * JB), ("conv_b_bias", JB), ("ln_b_g", JB),
                    ("ln_b_b", JB), ("g_q", 1), ("g_k", 1), ("lam_q1", 1), ("lam_q2", 1), ("lam_k1", 1),
                    ("lam_k2", 1), ("g_subln", 1), ("conv_d", 3 * 3 * JB), ("hf_bias", JB), ("hf_b1", 1),
                    ("hf_freq", 1), ("hf_b2", 1), ("w_router", 2 * KB * NE))
LVEC, NLVEC = columns(("ffn1_norm", KB), ("mix_norm", KB), ("ffn2_norm", KB), ("b_gate", 2 * KB),
                      ("na_q_norm", 1), ("na_k_norm", 1), ("sw_q_norm", 1), ("sw_k_norm", 1))
KEPT, NKEPT = columns(("ident", P), ("ones", P), ("halves", P), ("rope_swap", P), ("slot_no", CAP))
EARLY, NEARLY = columns(("z", T), ("decay", TT * AW), ("dft", TT * 2 * T))
MIDDLE, NMIDDLE = columns(("cos", T), ("sin", T), ("idft", 4 * T))
LATE, NLATE = columns(("na_mask", TT * T), ("sw_mask", TT * T), ("bucket", 2 * T))


def blocks(v):
    return np.ascontiguousarray(v.reshape(-1, P).T)


def padded(v):
    out = np.zeros((P, v.shape[1]), np.float32)
    out[:v.shape[0]] = v
    return out


def twice(v):
    return np.concatenate([v, v]).reshape(P, 1)


def pack_vectors(a):
    col = {"c": blocks(a["c"]), "c_ctx": blocks(a["c_ctx"]), "b_ada": blocks(a["b_ada"]),
           "g_mix": blocks(a["g_mix"]), "g_ffn": blocks(a["g_ffn"]), "conv_a": blocks(a["conv_a"]),
           "conv_b": blocks(a["conv_b"]), "conv_b_bias": blocks(a["conv_b_bias"]), "ln_b_g": blocks(a["ln_b_g"]),
           "ln_b_b": blocks(a["ln_b_b"]), "g_q": twice(a["g_q"][0]), "g_k": twice(a["g_k"][0]),
           "g_subln": blocks(a["g_subln"]), "conv_d": blocks(a["conv_d"]), "hf_bias": blocks(a["hf_bias"])}
    for n in ("lam_q1", "lam_q2", "lam_k1", "lam_k2", "hf_b1", "hf_freq", "hf_b2"):
        col[n] = padded(a[n][0].reshape(-1, 1))
    col["w_router"] = a["w_router"].reshape(2, KB, P, NE).transpose(2, 0, 1, 3).reshape(P, -1)
    return np.ascontiguousarray(np.concatenate([col[n] for n in VEC], axis=1))


def pack_layer_vectors(a):
    lots = []
    for l in range(LAYERS):
        col = {n: blocks(a[n + "_2"][l]) for n in ("ffn1_norm", "mix_norm", "ffn2_norm", "b_gate")}
        col |= {n: twice(a[n + "_2"][l]) for n in ("na_q_norm", "na_k_norm", "sw_q_norm", "sw_k_norm")}
        lots.append(np.concatenate([col[n] for n in LVEC], axis=1))
    return np.ascontiguousarray(np.concatenate(lots, axis=1))


def by_rows(m):
    n = m.shape[0] // P
    return m.reshape(n, P, -1).transpose(1, 0, 2).reshape(P, -1)


def kept_constants():
    halves = np.kron(np.eye(2), np.ones((DH, DH)))
    swap = np.zeros((P, P))
    for f in range(P):
        swap[f ^ 16, f] = 1.0
    slot_no = np.tile(np.arange(CAP), (P, 1))
    return np.concatenate([np.eye(P), np.ones((P, P)), halves, swap, slot_no], axis=1).astype(np.float32)


def early_constants():
    f32 = np.float32
    t = np.arange(T, dtype=f32)
    bands = np.linspace(1e-4, 15, 16, dtype=f32)
    ang = ((f32(TWO_PI / T) * t)[:, None] * bands[None]).astype(np.float64)
    z = np.concatenate([np.linspace(0.0, 1.0, T)[:, None], np.cos(ang), -np.sin(ang)], axis=1)
    dist = np.abs(t - T // 2) / (T // 2)
    rate = np.abs(np.linspace(math.log(1e-2) / 1.5, math.log(1e-2) / 0.3, AW))
    decay = np.exp(-dist[:, None].astype(np.float64) * rate[None])
    ph = np.pi * np.outer(np.arange(T), np.arange(T) + 0.5) / T
    dft = np.concatenate([np.cos(ph), -np.sin(ph)], axis=1)
    return np.concatenate([padded(z.T), by_rows(decay), by_rows(dft)], axis=1).astype(f32)


def middle_constants():
    f32 = np.float32
    inv = (f32(10000.0) ** (-np.arange(16, dtype=f32) / f32(16))).astype(f32)
    tok = np.arange(T)
    row, col = (tok // GRID).astype(f32), (tok % GRID).astype(f32)
    f = np.arange(P) % DH
    ang = np.where((f < 32)[:, None], row[None], col[None]).astype(f32) * inv[f % 16][:, None]
    ang = ang.astype(f32).astype(np.float64)
    cos, sin = np.cos(ang), np.sin(ang) * np.where((f % 32 < 16), -1.0, 1.0)[:, None]
    ph = np.pi * np.outer(np.arange(T) + 0.5, np.arange(T) + T // 2) / T
    idft = np.concatenate([np.cos(ph), -np.sin(ph)], axis=0) / T
    return np.concatenate([cos, sin, by_rows(idft)], axis=1).astype(f32)


def late_constants():
    q, k = np.arange(T)[:, None], np.arange(T)[None]
    start = np.clip(q % GRID - 8, 0, GRID - 16)
    na = np.where((k % GRID >= start) & (k % GRID < start + 16), 0.0, NEG)
    sw = np.where(np.abs(k - q) <= P, 0.0, NEG)
    rel = np.arange(2 * T) - (T - 1)
    n = np.abs(rel)
    large = np.minimum(8 + (np.log(np.maximum(n, 1) / 8) / np.log(128 / 8) * 8).astype(np.int32), 15)
    bucket = (rel > 0) * 16 + np.where(n < 8, n, large)
    hot = (np.arange(32)[:, None] == bucket[None]).astype(np.float32)
    return np.concatenate([by_rows(na)[::-1], by_rows(sw)[::-1], padded(hot)], axis=1).astype(np.float32)


class Count:

    def __init__(self, nc, name, unit=1):
        self.name, self.unit, self.n, self.loop = name, unit, 0, None
        self.sem = nc.alloc_semaphore(name)

    def step(self, ins, steps=1):
        ins.then_inc(self.sem, self.unit * steps)
        self.n += steps
        return self.here()

    def here(self):
        return Mark(self, self.n, self.loop)


class Mark:

    def __init__(self, count, n, loop=None):
        self.count, self.n, self.loop = count, n, loop

    def value(self, turn=None):
        steps = self.n if self.loop is None else self.n + self.loop.stride[self.count.name] * turn
        return steps * self.count.unit


class Loop:

    def __init__(self, name, turns, stride):
        self.name, self.turns, self.stride, self.made = name, turns, stride, {}


class Queue:

    def __init__(self, nc, eng, name):
        self.eng, self.name = eng, name
        self.count = Count(nc, f"{name}_done")
        self.counts = [self.count]
        self.past, self.past_turn = {}, {}
        self.turn, self.loop = None, None

    def after(self, *marks, turn=None):
        for m in marks:
            if m is None:
                continue
            if isinstance(m, (list, tuple)):
                self.after(*m, turn=turn)
                continue
            if m.loop is None:
                v = m.value()
                if v == 0:
                    continue
                if self.past.get(m.count, 0) >= v or (m.count in self.past_turn):
                    continue
                self.past[m.count] = v
            elif turn is not None:
                v = m.value(turn)
            elif m.loop is self.loop:
                if self.past_turn.get(m.count, 0) >= m.n:
                    continue
                self.past_turn[m.count] = m.n
                v = m.value(self.turn)
            else:
                v = m.value(m.loop.turns - 1)
                if self.past.get(m.count, 0) >= v:
                    continue
                self.past[m.count] = v
            self.eng.wait_ge(m.count.sem, v)

    def done(self, ins):
        return self.count.step(ins)

    def last(self):
        return [c.here() for c in self.counts]


@contextmanager
def turns_of(nc, name, turns, queues, counts, known, made):
    loop = Loop(name, turns, known.get(name) or {c.name: 1 for c in counts})
    base = {c: c.n for c in counts}
    engines = tuple({"pe": ET.PE, "act": ET.Activation, "dve": ET.DVE, "pool": ET.Pool,
                     "sp": ET.SP}[q.name] for q in queues)
    for c in counts:
        c.loop = loop
    with nc.Fori(0, turns, engines=engines) as i:
        for q in queues:
            q.turn, q.loop, q.past_turn = i, loop, {}
        yield loop, i
        for q in queues:
            q.turn, q.loop, q.past_turn = None, None, {}
    loop.stride = made[name] = {c.name: c.n - base[c] for c in counts}
    for c in counts:
        c.loop = None
        c.n = base[c] + loop.stride[c.name] * turns


def program(nc, a, out, known):
    made = {}

    def hold(name, floats):
        return nc.alloc_sbuf_tensor(f"sb_{name}", [P, floats], F32)

    pe, act, dve = Queue(nc, nc.tensor, "pe"), Queue(nc, nc.scalar, "act"), Queue(nc, nc.vector, "dve")
    pool, sp = Queue(nc, nc.gpsimd, "pool"), Queue(nc, nc.sync, "sp")
    workers = [pe, act, dve, pool]

    ring = hold("ring", SLOTS * SLOT)
    H = hold("hidden", NS * KB * T)[:, :].rearrange("p (s k t) -> p s k t", s=NS, k=KB)
    U = hold("normed", NS * KB * T)[:, :].rearrange("p (s k t) -> p s k t", s=NS, k=KB)
    vec_mem, kept_mem = hold("vectors", NVEC), hold("kept", NKEPT)
    lvec_mem, cur = hold("layer_vectors", LAYERS * NLVEC), hold("layer_now", NLVEC)
    sink_mem = hold("sinks", LAYERS * SW_H)
    mod_mem = hold("modulation", 2 * 6 * KB * NS)
    MOD = mod_mem[:, :].rearrange("p (l c k s) -> p l c k s", l=2, c=6, k=KB)
    fold_mem = hold("folded_gains", 2 * 2 * KB * NS)
    FOLD = fold_mem[:, :].rearrange("p (l n k s) -> p l n k s", l=2, n=2, k=KB)
    small = hold("small", 256)
    eps_columns = hold("epsilons", 2)[:, :]
    MAIN, SUB = 0, 1
    arena = hold("arena", ARENA)
    banks = [nc.alloc_psum_tensor(f"bank{b}", [P, 512], F32) for b in range(8)]
    bank_read = [None] * 8

    def vec(name, i=0, n=1):
        c = VEC[name][0] + i
        return vec_mem[:, c:c + n]

    def kept(name):
        c, n = KEPT[name]
        return kept_mem[:, c:c + n]

    ident, ones, halves = kept("ident"), kept("ones"), kept("halves")

    class Carve:

        def __init__(self, at=0, end=ARENA, mem=None):
            self.at, self.end, self.mem = at, end, arena[:, :] if mem is None else mem

        def __call__(self, *shape):
            n = math.prod(shape)
            self.at += n
            assert self.at <= self.end, (self.at, self.end)
            part = self.mem[:, self.at - n:self.at]
            if len(shape) == 1:
                return part
            names = "abcd"[:len(shape)]
            return part.rearrange(f"p ({' '.join(names)}) -> p {' '.join(names)}", **dict(zip(names, shape)))

    landed = [Count(nc, f"landed{s}", 16) for s in range(SLOTS)]
    chunks_read = Count(nc, "chunks_read")
    pe.counts.append(chunks_read)
    issued = [0]

    def fetch(src):
        slot, k = issued[0] % SLOTS, src.shape[0] // P
        issued[0] += 1
        if issued[0] > SLOTS:
            sp.after(Mark(chunks_read, issued[0] - SLOTS, chunks_read.loop))
        tile = ring[:, slot * SLOT:(slot + 1) * SLOT].rearrange("p (k n) -> p k n", k=k)
        return tile, landed[slot].step(nc.sync.dma_start(tile, src.rearrange("(k p) n -> p k n", p=P)))

    def meet():
        marks = [q.last() for q in (pe, act, dve)]
        for q in workers:
            q.after(marks)

    def mm(o, lhsT, rhs, start, stop):
        return nc.tensor.matmul(o, lhsT, rhs, start=start, stop=stop, skip_group_check=True)

    def turn_over(o, x, *marks):
        pe.after(*marks)
        return nc.tensor.transpose(o, x, ident[0:x.shape[0], 0:x.shape[0]])

    def A(o, x, func, *marks, bias=None, scale=None, accum=None):
        act.after(*marks)
        kw = {}
        if bias is not None:
            kw["bias"] = bias
        if scale is not None:
            kw["scale"] = scale
        if accum is not None:
            kw["accum_out"] = accum
        return act.done(nc.scalar.activation(o, x, func, **kw))

    def copy_a(o, x, *marks):
        act.after(*marks)
        return act.done(nc.scalar.copy(o, x))

    def copy_v(o, x, *marks):
        dve.after(*marks)
        return dve.done(nc.vector.tensor_copy(o, x))

    def TS(o, x, s1, op0, s2=None, op1=None, marks=()):
        dve.after(*marks)
        if s2 is None:
            return dve.done(nc.vector.tensor_scalar(o, x, s1, None, op0))
        return dve.done(nc.vector.tensor_scalar(o, x, s1, s2, op0, op1))

    def STT(o, x, s, y, op0, op1, marks=()):
        dve.after(*marks)
        return dve.done(nc.vector.scalar_tensor_tensor(out=o, in0=x, scalar=s, in1=y, op0=op0, op1=op1))

    def VV(o, x, y, op, marks=()):
        dve.after(*marks)
        return dve.done(nc.vector.tensor_tensor(o, x, y, op))

    def RED(o, x, op, marks=(), negate=False):
        dve.after(*marks)
        return dve.done(nc.vector.tensor_reduce(o, x, AX.X, op, negate=negate))

    def RECIP(o, x, *marks):
        dve.after(*marks)
        return dve.done(nc.vector.reciprocal(o, x))

    def fill(o, value, *marks):
        dve.after(*marks)
        return dve.done(nc.vector.memset(o, value))

    def load(count, dst, src, q=act, after=()):
        q.after(*after)
        return count.step(q.eng.dma_start(dst, src))

    def counted(name):
        return Count(nc, name, 16)

    m_vec = load(counted("in_vectors"), vec_mem[:, :], a["vectors"])
    m_kept = load(counted("in_kept"), kept_mem[:, :], a["kept"])
    carve = Carve(0, ARENA - NMIDDLE - 2048 - TT * 2 * T)
    cond = small[:, :].rearrange("p (k m) -> p k m", k=KB)
    ada_row, ada_turned = carve(512), carve(32)
    ADA_END = carve.at
    top = Carve(carve.end)
    BLOCK1_END = top.at
    dft = top(TT, 2 * T)
    HF = top(4, AW)
    COS, SIN, idft = top(T), top(T), top(4, T)
    m_x = load(counted("in_x"), H[:, 0], a["x_t"].rearrange("(k p) t -> p k t", p=P), sp)
    m_ctx = load(counted("in_ctx"), H[:, 1], a["ctx_t"].rearrange("(k p) t -> p k t", p=P), sp)

    fill(eps_columns[:, MAIN:MAIN + 1], EPS)
    m_eps = fill(eps_columns[:, SUB:SUB + 1], SUB_EPS)
    m = fill(cond, 0.0)
    A(cond[:, :, 0], vec("c", 0, KB), ACT.Silu, m, m_vec)
    m_cond = A(cond[:, :, 1], vec("c_ctx", 0, KB), ACT.Silu)
    ADA_BANK, TURN_BANK = 6, 7
    turned_read = [None]

    def ada(l, pair):
        return list(ada_steps(l, pair))[-1]

    def ada_steps(l, pair):
        bank = banks[ADA_BANK]
        pe.after(m_cond)
        pe.after(bank_read[ADA_BANK])
        for h in range(2):
            c0 = D * (2 * pair + h)
            for r in range(KB // 2):
                w, there = fetch(a["w_ada"][l, 2 * P * r:2 * P * (r + 1), c0:c0 + D])
                pe.after(there)
                for kk in range(2):
                    k = 2 * r + kk
                    for half in range(2):
                        j = 2 * h + half
                        ins = mm(bank[32 * j:32 * j + 32, :], cond[:, k, :],
                                 w[:, kk, 512 * half:512 * half + 512], k == 0, k == KB - 1)
                m = chunks_read.step(ins)
            if h == 0:
                yield
        m = bank_read[ADA_BANK] = copy_a(ada_row, bank[:, :], m)
        pe.after(bank_read[TURN_BANK])
        for c in range(4):
            ins = turn_over(banks[TURN_BANK][:, P * c:P * c + P], ada_row[:, P * c:P * c + P], m, m_kept)
        turned = ada_turned.rearrange("p (c j s) -> p c j s", c=4, j=4)
        m = bank_read[TURN_BANK] = copy_a(turned, banks[TURN_BANK][:, :].rearrange("p (c j m) -> p c j m", c=4, j=4)[:, :, :, 0:NS],
                                          pe.done(ins), turned_read[0])
        yield
        for j in range(4):
            sec, k = 2 * pair + j // 2, 4 * (j % 2)
            bias = vec("b_ada", (l * 6 + sec) * KB + k, 4).rearrange("p (k o) -> p k o", o=1).broadcast_to([P, 4, NS])
            done = VV(MOD[:, l, sec, k:k + 4, :], turned[:, :, j, :], bias, ALU.add, marks=[m, m_vec])
        turned_read[0] = done
        yield done

    def fold(l, n, m):
        g = vec("g_ffn" if n else "g_mix", l * KB, KB)
        for s in range(NS):
            m = STT(FOLD[:, l, n, :, s], MOD[:, l, 3 * n + 1, :, s], 1.0, g, ALU.add, ALU.mult, marks=[m])
        return m

    def inverse_rms(o, total, scale, eps, m):
        read = A(o, total, ACT.Sqrt, m, m_eps, bias=eps_columns[:, eps:eps + 1], scale=scale)
        return read, RECIP(o, o, read)

    def sum_squares(b, streams, sq, ready=None):
        w, lo, read = len(streams) * T, streams[0], [None, None]
        pe.after(bank_read[b])
        for k in range(KB):
            part = sq[:, 512 * (k % 2):512 * (k % 2) + w]
            pe.after(A(part.rearrange("p (s t) -> p s t", t=T), H[:, lo:lo + len(streams), k, :], ACT.Square,
                       read[k % 2], ready and ready[k]))
            read[k % 2] = pe.done(mm(banks[b][:, 0:w], ones, part, k == 0, k == KB - 1))
        return read[1]

    def inverse_root(b, w, rinv, m):
        bank_read[b], m = inverse_rms(rinv[:, 0:w], banks[b][:, 0:w], 1.0 / D, MAIN, m)
        return m

    def rms(b, streams, sq, rinv):
        return inverse_root(b, len(streams) * T, rinv, sum_squares(b, streams, sq))

    def modulated(l, n, streams, rinv, m):
        out = []
        for k in range(KB):
            for i, s in enumerate(streams):
                v = STT(U[:, s, k, :], H[:, s, k, :], FOLD[:, l, n, k, s:s + 1], rinv[:, i * T:i * T + T],
                        ALU.mult, ALU.mult, marks=[m])
                v = A(U[:, s, k, :], U[:, s, k, :], ACT.Identity, v, bias=MOD[:, l, 3 * n, k, s:s + 1])
            out.append(v)
        return out

    def columns_of(w, c0, n=SLOT // KB):
        return w[:, c0:c0 + n]

    sq, rinv, mean = carve(1024), carve(512), carve(512)
    GI, SG, CA = carve(512), carve(512), carve(512)
    PA, PB = carve(NS, T + 2), carve(NS, T + TAPS_B - 1)
    Z = carve(JB, NS * T)
    Y = carve(KB, NS * T)
    act.after(m_x, m_ctx)
    dve.after(m_x, m_ctx)
    pe.after(m_kept)
    m_rms = rms(5, (0, 1), sq, rinv)
    fold(0, 0, ada(0, 0))
    u_ready = modulated(0, 0, (0, 1), rinv, [m_rms, dve.last()])

    z, turns, arg, hid = carve(T), carve(T), carve(T), carve(T)
    fw1, fw2, fw3 = carve(64), carve(64), carve(AW)
    decay, htok = Y[:, JB:JB + TT, :], Y[:, JB + TT:KB, :]
    e = EARLY["decay"][0], EARLY["dft"][0]
    in_filter = counted("in_filter")
    load(in_filter, fw1[0:33, :], a["hf_w1"][0])
    load(in_filter, fw2[0:64, :], a["hf_w2"][0])
    load(in_filter, fw3[0:64, :], a["hf_w3"][0])
    load(in_filter, z, a["early"][:, 0:e[0]])
    load(in_filter, decay.rearrange("p t n -> p (t n)"), a["early"][:, e[0]:e[1]])
    m_filter = load(in_filter, dft.rearrange("p t n -> p (t n)"), a["early"][:, e[1]:])
    in_middle = counted("in_middle")
    load(in_middle, COS, a["middle"][:, 0:T])
    load(in_middle, SIN, a["middle"][:, T:2 * T])
    m_middle = load(in_middle, idft.rearrange("p b t -> p (b t)"), a["middle"][:, 2 * T:])
    in_layers = counted("in_layer_vectors")
    load(in_layers, lvec_mem[:, :], a["layer_vectors"])
    m_layers = load(in_layers, sink_mem[:, :], bass.AP(tensor=a["sw_sink_2"].tensor, offset=0,
                                                        ap=[[0, P], [1, LAYERS * SW_H]]))

    def sine(o, x, m):
        hi = 6.28125
        m = TS(turns[0:64, :], x, 1.0 / TWO_PI, ALU.mult, ROUND, ALU.add, marks=[m])
        m = TS(turns[0:64, :], turns[0:64, :], ROUND, ALU.subtract, marks=[m])
        m = STT(x, turns[0:64, :], -hi, x, ALU.mult, ALU.add, marks=[m])
        m = STT(x, turns[0:64, :], hi - TWO_PI, x, ALU.mult, ALU.add, marks=[m])
        m = TS(x, x, 3.1415925, ALU.min, -3.1415925, ALU.max, marks=[m])
        return A(o, x, ACT.Sin, m)

    def long_filter():
        freq = vec("hf_freq")[0:64, :]
        m = m_filter
        for w, rows, x, bias in ((fw1, 33, z, "hf_b1"), (fw2, 64, hid, "hf_b2")):
            pe.after(m, bank_read[5])
            m = pe.done(mm(banks[5][0:64, 0:T], w[0:rows, 0:64], x[0:rows, :], True, True))
            m = bank_read[5] = TS(arg[0:64, :], banks[5][0:64, 0:T], vec(bias)[0:64, :], ALU.add, freq, ALU.mult,
                                  marks=[m, m_vec])
            m = sine(hid[0:64, :], arg[0:64, :], m)
            yield
        pe.after(m)
        for t in range(TT):
            pe.after(bank_read[5 + t])
            m = pe.done(mm(banks[5 + t][:, :], hid[0:64, t * P:t * P + P], fw3[0:64, :], True, True))
            m = bank_read[5 + t] = VV(htok[:, t, :], banks[5 + t][:, :], decay[:, t, :], ALU.mult, marks=[m, m_filter])
        yield
        pe.after(m)
        for f in range(4):
            b = 5 + f % 2
            pe.after(bank_read[b])
            for t in range(TT):
                ins = mm(banks[b][:, :], dft[:, t, f * P:f * P + P], htok[:, t, :], t == 0, t == TT - 1)
            bank_read[b] = copy_a(HF[:, f, :], banks[b][:, :], pe.done(ins))
        yield

    filter_steps = long_filter()
    fill(PA, 0.0)
    m_pads = fill(PB, 0.0)
    ada_done = {}
    w_in = a["w_in_ab"][0]
    GROUP = {"gate_out": 0, "gate_in": 1, "val": 2, "glu_a": 3, "glu_g": 4}
    both = lambda x: x.rearrange("p (s t) -> p s t", s=NS)

    def tap(name, k, j):
        return vec(name, k * JB + j)

    for jp in range(JB // 2):
        w = {g: fetch(columns_of(w_in, AW * GROUP[g] + 256 * jp)) for g in ("gate_in", "val", "glu_g", "glu_a", "gate_out")}
        for jj in range(2):
            j, got = 2 * jp + jj, {}
            for b, (g, (tile, there)) in enumerate(w.items()):
                pe.after(there)
                pe.after(bank_read[b])
                for k in range(KB):
                    pe.after(u_ready[k])
                    ins = mm(both(banks[b][:, :]), tile[:, k, P * jj:P * jj + P], U[:, :, k, :], k == 0, k == KB - 1)
                got[g] = (chunks_read if jj else pe.count).step(ins)
                if g == "gate_in":
                    m_gi = bank_read[b] = copy_a(GI, banks[b][:, :], got[g], dve.last())
                elif g == "val":
                    m_pa = bank_read[b] = VV(PA[:, :, 1:T + 1], both(banks[b][:, :]), both(GI), ALU.mult,
                                             marks=[got[g], m_gi, m_pads, dve.last()])
                elif g == "glu_g":
                    m_sg = bank_read[b] = A(SG, banks[b][:, :], ACT.Sigmoid, got[g], dve.last())
                elif g == "glu_a":
                    m_pb = bank_read[b] = VV(PB[:, :, 15:T + 15], both(banks[b][:, :]), both(SG), ALU.mult,
                                             marks=[got[g], m_sg])
            next(filter_steps)
            m = TS(both(CA), PA[:, :, 0:T], tap("conv_a", 0, j), ALU.mult, marks=[m_pa])
            for k in range(1, TAPS_A):
                m = STT(both(CA), PA[:, :, k:k + T], tap("conv_a", k, j), both(CA), ALU.mult, ALU.add, marks=[m])
            bank_read[4] = VV(Y[:, j, :], CA, banks[4][:, :], ALU.mult, marks=[m, got["gate_out"]])
            z_j = both(Z[:, j, :])
            m = TS(z_j, PB[:, :, 0:T], tap("conv_b", 0, j), ALU.mult, vec("conv_b_bias", j), ALU.add, marks=[m_pb])
            for k in range(1, TAPS_B):
                m = STT(z_j, PB[:, :, k:k + T], tap("conv_b", k, j), z_j, ALU.mult, ALU.add, marks=[m])
        for pair in ((0, 1), (0, 2)) if jp == 0 else ((1, 0),):
            ada_done[pair] = ada(*pair)
    m_z = m
    beside = ada_steps(1, 1)
    next(beside)
    pe.after(m_z)
    pe.after(bank_read[0])
    for j in range(JB):
        ins = mm(banks[0][:, :], ones, Z[:, j, :], j == 0, j == JB - 1)
    m_mean = bank_read[0] = TS(mean, banks[0][:, :], 1.0 / AW, ALU.mult, marks=[pe.done(ins)])
    read = [None, None]
    pe.after(bank_read[1])
    for j in range(JB):
        m = VV(Z[:, j, :], Z[:, j, :], mean, ALU.subtract, marks=[m_mean])
        pe.after(A(sq[:, 512 * (j % 2):512 * (j % 2) + 512], Z[:, j, :], ACT.Square, m, read[j % 2]))
        read[j % 2] = pe.done(mm(banks[1][:, :], ones, sq[:, 512 * (j % 2):512 * (j % 2) + 512], j == 0, j == JB - 1))
    bank_read[1], m = inverse_rms(rinv, banks[1][:, :], 1.0 / AW, MAIN, read[1])
    next(beside)
    for j in range(JB):
        v = VV(Z[:, j, :], Z[:, j, :], rinv, ALU.mult, marks=[m])
        m_y = A(Y[:, JB + j, :], Z[:, j, :], ACT.Silu, v, bias=vec("ln_b_b", j), scale=vec("ln_b_g", j))
    next(beside)

    def project_back(w, rhs, l, streams, m):
        pe.after(m)
        for c in range(KB // 2):
            tile, there = fetch(columns_of(w, 256 * c))
            pe.after(there)
            for half in range(2):
                n, b = 2 * c + half, 2 + (2 * c + half) % 4
                pe.after(bank_read[b])
                w_ = len(streams) * T
                for k in range(KB):
                    ins = mm(banks[b][:, 0:w_], tile[:, k, P * half:P * half + P], rhs[:, k, :], k == 0, k == KB - 1)
                m = (chunks_read if half else pe.count).step(ins)
                for i, s in enumerate(streams):
                    bank_read[b] = STT(H[:, s, n, :], banks[b][:, i * T:i * T + T], MOD[:, l, 2, n, s:s + 1],
                                       H[:, s, n, :], ALU.mult, ALU.add, marks=[m])

    fold(0, 1, ada_done[0, 2])
    fold(1, 0, ada_done[1, 0])
    project_back(a["w_out_ab"][0], Y, 0, (0, 1), m_y)

    def moe(l, streams, sq, beside=()):
        S = len(streams)
        lo = streams[0]
        assert 3 * D * D == SLOTS * P * SLOT
        weights = [a["w_gate"], a["w_up"], a["w_down"]]

        def chunk(g, e, which, r):
            w, there = fetch(weights[which][l, g * EG + e, 2 * P * r:2 * P * (r + 1), :])
            pe.after(there)
            return w

        m_sum = sum_squares(7, streams, sq, [dve.last()] * KB)
        meet()
        carve = Carve(ADA_END, BLOCK1_END)
        U2T = carve(2 * S, D)
        OH = carve(2 * S, NE * CAP)
        OHW = carve(2 * S, NE * CAP)
        SW = carve(NE // EG, S * T)
        SG, HH, HT = carve(512), carve(512), carve(4, 2 * CAP * 2)
        AF, POS, tmp = carve(TT, S * NE), carve(TT, S * NE), carve(TT * S, NE)
        W0, W1, mask, cum = carve(T), carve(T), carve(T), carve(T)
        m8, ones_row = carve(8), carve(T)
        mx, sm = carve(TT * S), carve(TT * S)
        YG = OHW[:, 0:2 * S, :].rearrange("p (s h) n -> p s (h n)", s=S)
        rinv = HT.rearrange("p a b -> p (a b)")
        u_ready = modulated(l, 1, streams, rinv, inverse_root(7, S * T, rinv, m_sum))
        fill(ones_row, 1.0)
        pe.after(bank_read[0])
        for t in range(TT):
            for i, s in enumerate(streams):
                c = (t * S + i) * NE
                for k in range(KB):
                    pe.after(u_ready[k])
                    ins = mm(banks[0][:, c:c + NE], U[:, s, k, P * t:P * t + P],
                             vec("w_router", (l * KB + k) * NE, NE), k == 0, k == KB - 1)
        m = pe.done(ins)
        for i, s in enumerate(streams):
            for t in range(TT):
                for half in range(2):
                    b = 1 + (2 * t + half) % 4
                    pe.after(bank_read[b])
                    for c in range(4):
                        ins = turn_over(banks[b][:, P * c:P * c + P], U[:, s, 4 * half + c, P * t:P * t + P])
                    m_turn = bank_read[b] = copy_a(U2T[:, 2 * i + t, 512 * half:512 * half + 512], banks[b][:, :],
                                                   pe.done(ins), u_ready[-1])
        for step in beside[0:1]:
            step()
        logits = banks[0][:, 0:TT * S * NE].rearrange("p (a e) -> p a e", e=NE)
        af = AF.rearrange("p t (s e) -> p (t s) e", e=NE)
        wide = lambda x: x.rearrange("p (a o) -> p a o", o=1).broadcast_to([P, TT * S, NE])
        m = RED(mx, logits, ALU.max, marks=[m])
        m = bank_read[0] = VV(tmp, logits, wide(mx), ALU.subtract, marks=[m])
        m = A(tmp, tmp, ACT.Exp, m)
        m = RED(sm, tmp, ALU.add, marks=[m])
        m = RECIP(sm, sm, m)
        m_af = VV(af, tmp, wide(sm), ALU.mult, marks=[m])
        R = S * NE
        pe.after(bank_read[5])
        for t in range(TT):
            ins = turn_over(banks[5][0:R, P * t:P * t + P], AF[:, t, :], m_af)
        m = bank_read[5] = copy_v(W0[0:R, :], banks[5][0:R, 0:T], pe.done(ins))
        for step in beside[1:2]:
            step()
        src, dst = W0, W1
        for _ in range(CAP // 8):
            dve.after(m)
            m = dve.done(nc.vector.max(m8[0:R, :], src[0:R, :]))
            dve.after(m)
            m = dve.done(nc.vector.match_replace(dst[0:R, :], m8[0:R, :], src[0:R, :], -1.0))
            src, dst = dst, src
        m = TS(mask[0:R, :], src[0:R, :], 0.0, ALU.is_lt, marks=[m])
        dve.after(m)
        m = dve.done(nc.vector.tensor_tensor_scan(cum[0:R, :], ones_row[0:R, :], mask[0:R, :], 0.0, ALU.mult, ALU.add))
        m = VV(cum[0:R, :], cum[0:R, :], mask[0:R, :], ALU.mult, marks=[m])
        m = TS(cum[0:R, :], cum[0:R, :], -1.0, ALU.add, marks=[m])
        pe.after(bank_read[6])
        for t in range(TT):
            ins = turn_over(banks[6][:, R * t:R * t + R], cum[0:R, P * t:P * t + P], m)
        m = bank_read[6] = copy_v(POS.rearrange("p t r -> p (t r)"), banks[6][:, 0:TT * R], pe.done(ins))
        for step in beside[2:]:
            step()
        slot_no = kept("slot_no").rearrange("p (o j) -> p o j", o=1).broadcast_to([P, NE, CAP])
        for i in range(S):
            for t in range(TT):
                at = lambda x: x[:, t, NE * i:NE * i + NE].rearrange("p (e o) -> p e o", o=1).broadcast_to([P, NE, CAP])
                hot = lambda x: x[:, 2 * i + t, :].rearrange("p (e j) -> p e j", j=CAP)
                m_oh = VV(hot(OH), slot_no, at(POS), ALU.is_equal, marks=[m])
                m_ohw = VV(hot(OHW), hot(OH), at(AF), ALU.mult, marks=[m_oh])
        for g in range(NE // EG):
            b = 1 + g
            pe.after(bank_read[b])
            for i in range(S):
                for t in range(TT):
                    ins = turn_over(banks[b][:, (2 * i + t) * P:(2 * i + t + 1) * P], OHW[:, 2 * i + t, P * g:P * g + P], m_ohw)
            bank_read[b] = copy_a(SW[:, g, :], banks[b][:, 0:S * T], pe.done(ins))
        GATE, UP, TURN, DOWN, OUT = 0, 1, 3, 4, 5
        XE = U[:, 0].rearrange("p k (e m) -> p k e m", e=EG)
        fill(XE, 0.0, m_turn)
        swf = SW.rearrange("p g n -> p (g n)")
        with turns_of(nc, f"experts{l}", NE // EG, [*workers, sp],
                      [*(q.count for q in workers), chunks_read, *landed], known, made) as (loop, g):
            meet()
            m_xe = []
            for q, b in enumerate((2, 5, 6, 7)):
                for k in (2 * q, 2 * q + 1):
                    for i in range(S):
                        c = S * P * (k % 2) + P * i
                        for t in range(TT):
                            ins = mm(banks[b][:, c:c + P], U2T[:, 2 * i + t, P * k:P * k + P],
                                     OH[:, 2 * i + t, bass.ds(g * P, P)], t == 0, t == TT - 1)
                m = pe.done(ins)
                for k in (2 * q, 2 * q + 1):
                    got = banks[b][:, S * P * (k % 2):S * P * (k % 2) + S * P].rearrange("p (i e j) -> p i e j", i=S, e=EG)
                    to = XE[:, k].rearrange("p e (i j) -> p i e j", i=NS)[:, 0:S]
                    m_xe.append((copy_v if q % 2 else copy_a)(to, got, m))
            read = {b: m_xe for b in range(8)}

            for e in range(EG):
                for which, b in ((0, GATE), (1, UP)):
                    if e > 0:
                        pe.after(read[b])
                    for r in range(KB // 2):
                        w = chunk(g, e, which, r)
                        for kk in range(2):
                            k = 2 * r + kk
                            pe.after(m_xe[k])
                            for half in range(2):
                                ins = mm(banks[b][64 * half:64 * half + 64, :], XE[:, k, e, :],
                                         w[:, kk, 512 * half:512 * half + 512], k == 0, k == KB - 1)
                        m = chunks_read.step(ins)
                    if which == 0:
                        m_sg = read[b] = A(SG, banks[b][:, :], ACT.Silu, m, dve.last())
                    else:
                        m_hh = read[b] = VV(HH, banks[b][:, :], SG, ALU.mult, marks=[m, m_sg])
                pe.after(read[TURN])
                for c in range(4):
                    ins = turn_over(banks[TURN][:, P * c:P * c + P], HH[:, P * c:P * c + P], m_hh)
                m_ht = read[TURN] = copy_v(HT.rearrange("p a b -> p (a b)"), banks[TURN][:, :], pe.done(ins))
                pe.after(m_ht, read[DOWN])
                for r in range(KB // 2):
                    w = chunk(g, e, 2, r)
                    for kk in range(2):
                        k = 2 * r + kk
                        half, c = divmod(k, 4)
                        for out_half in range(2):
                            ins = mm(banks[DOWN][64 * out_half:64 * out_half + 64, :], HT[:, c, 64 * half:64 * half + 64],
                                     w[:, kk, 512 * out_half:512 * out_half + 512], k == 0, k == KB - 1)
                    m = chunks_read.step(ins)
                for i in range(S):
                    for out_half, copy in ((0, copy_a), (1, copy_v)):
                        p0 = 64 * out_half + CAP * i
                        m_c = copy(YG[CAP * e:CAP * e + CAP, i, 512 * out_half:512 * out_half + 512],
                                   banks[DOWN][p0:p0 + CAP, :], m)
                read[DOWN] = (act.last(), dve.last())
            pe.after(act.last(), dve.last())
            for n in range(KB):
                b = OUT + n % 3
                if n >= 3:
                    pe.after(read[b])
                for i in range(S):
                    ins = mm(banks[b][:, T * i:T * i + T], YG[:, i, P * n:P * n + P],
                             swf[:, bass.ds(g * (S * T) + T * i, T)], True, True)
                m = pe.done(ins)
                for i, s in enumerate(streams):
                    read[b] = STT(H[:, s, n, :], banks[b][:, T * i:T * i + T], MOD[:, l, 5, n, s:s + 1], H[:, s, n, :],
                                  ALU.mult, ALU.add, marks=[m])
        issued[0] = chunks_read.n
        for b in range(8):
            bank_read[b] = [act.last(), dve.last()]

    last_ada = ada_steps(1, 2)
    moe(0, (0, 1), sq, beside=(lambda: next(last_ada), lambda: next(last_ada), lambda: fold(1, 1, next(last_ada))))

    meet()
    carve = Carve(0, BLOCK1_END)
    Q, K = carve(HEADS, T), carve(HEADS, NS * T)
    V = carve(NS * TT, HEADS * P)
    at_var = carve.at
    var = carve(3072)
    reuse = Carve(at_var, at_var + 3072)
    Y, PT = reuse(KB, T), reuse(2 * TT, TT * P)
    PROD, GO = carve(JB, T), carve(JB, T)
    UT = carve(TT, AW)
    sq = carve(1024)
    rinv = carve(512)
    pad, gated = carve(2, T + 2), UT[:, 0, :]
    t1, t2 = sq[:, 0:512], sq[:, 512:1024]
    head_stats, lam, gq8, gsub = carve(2, 16), carve(4), carve(1), carve(1)
    u_ready = modulated(1, 0, (0, 1), rinv, rms(7, (0, 1), sq, rinv))
    ctx_u = U[:, 1].rearrange("p k t -> p (k t)")
    ctx_h = H[:, 1].rearrange("p k t -> p (k t)")
    exps = [x.rearrange("p (b n) -> p b n", b=4) for x in (ctx_u, U[:, 0].rearrange("p k t -> p (k t)"))]
    UF = ctx_h.rearrange("p (b n) -> p b n", b=4)
    w_in = a["w_in_cd"][0]
    m = VV(lam[:, 0:2], vec("lam_q1", 0, 2), vec("lam_k1", 0, 2), ALU.mult)
    m_gq = TS(gq8, vec("g_q"), DH ** -0.5, ALU.mult)
    m_gsub = TS(gsub, vec("g_subln"), 1.0 - LAM_INIT, ALU.mult)
    pe.after(bank_read[6])
    pe.after(m)
    m = pe.done(mm(banks[6][:, 0:2], ones, lam[:, 0:2], True, True))
    m = bank_read[6] = A(lam[:, 2:4], banks[6][:, 0:2], ACT.Exp, m)
    m_lam = STT(lam[:, 0:1], lam[:, 2:3], LAM_INIT, lam[:, 3:4], ALU.add, ALU.subtract, marks=[m])

    def rope(x, b, tmp, m):
        pe.after(bank_read[b])
        pe.after(m)
        m = pe.done(mm(banks[b][:, 0:T], kept("rope_swap"), x, True, True))
        m = bank_read[b] = VV(tmp, banks[b][:, 0:T], SIN, ALU.mult, marks=[m, m_middle, dve.last()])
        m2 = VV(x, x, COS, ALU.mult, marks=[pe.last()])
        return VV(x, x, tmp, ALU.add, marks=[m, m2])

    to_norm, to_rope = [], []

    def catch_up(everything=False):
        while to_rope:
            to_rope.pop(0)()
        while to_norm:
            to_norm.pop(0)()
        if everything:
            catch_up()

    def norm_heads(x, h, b, n, at, gain, m):
        flat, inv, b2 = sq[:, 512 * (h % 2):512 * (h % 2) + n], var[:, at:at + n], 4 + h % 2
        m = bank_read[b] = A(flat, banks[b][:, 0:n], ACT.Square, m, pe.last())
        pe.after(bank_read[b2], m)
        m = pe.done(mm(banks[b2][:, 0:n], halves, flat, True, True))
        bank_read[b2], m = inverse_rms(inv, banks[b2][:, 0:n], 1.0 / DH, MAIN, m)
        m = STT(x, x, gain, inv, ALU.mult, ALU.mult, marks=[m, m_gq])
        to_rope.append(lambda: roped.append(rope(x[:, 0:T], 6 + h % 2, rinv[:, T * (h % 2):T * (h % 2) + T], m)))

    def project_heads(c0, dst, var_at, rhs, n, gain):
        for c in range(2):
            tile, there = fetch(columns_of(w_in, c0 + 256 * c))
            pe.after(there)
            for half in range(2):
                h = b = 2 * c + half
                pe.after(bank_read[b])
                for k in range(KB):
                    pe.after(u_ready[k])
                    ins = mm(banks[b][:, 0:n], tile[:, k, P * half:P * half + P], rhs(k), k == 0, k == KB - 1)
                m = (chunks_read if half else pe.count).step(ins)
                catch_up()
                m = bank_read[b] = copy_a(dst[:, h, :], banks[b][:, 0:n], m)
                to_norm.append(lambda h=h, b=b, m=m: norm_heads(dst[:, h, :], h, b, n, var_at + h * n, gain, m))

    roped = []
    project_heads(512, K, 1024, lambda k: U[:, :, k, :], 512, vec("g_k"))
    tiles = [fetch(columns_of(w_in, 1024 + 256 * c)) for c in range(2)]
    for s in range(NS):
        for t in range(TT):
            b = 6 + t
            pe.after(bank_read[b])
            for c, (tile, there) in enumerate(tiles):
                pe.after(there)
                for k in range(KB):
                    ins = mm(banks[b][:, 256 * c:256 * c + 256], U[:, s, k, P * t:P * t + P], tile[:, k, :],
                             k == 0, k == KB - 1)
            m_v = chunks_read.step(ins, 2) if (s, t) == (NS - 1, TT - 1) else pe.done(ins)
            m_vcopy = bank_read[b] = copy_v(V[:, 2 * s + t, :], banks[b][:, :], m_v)
            catch_up()
    project_heads(0, Q, 0, lambda k: U[:, 0, k, :], T, gq8)

    def short_conv(c):
        for n, (first, dst) in enumerate(((512, PROD), (1024, None), (0, GO))):
            tile, there = fetch(columns_of(w_in, 1536 + first + 256 * c))
            b = 6 + n % 2
            pe.after(there)
            pe.after(bank_read[b])
            for half in range(2):
                for k in range(KB):
                    ins = mm(banks[b][:, T * half:T * half + T], tile[:, k, P * half:P * half + P], U[:, 0, k, :],
                             k == 0, k == KB - 1)
            m = chunks_read.step(ins)
            m = bank_read[b] = copy_a(pad[:, :, 1:T + 1], banks[b][:, :].rearrange("p (c t) -> p c t", c=2), m, dve.last())
            for half in range(2):
                blk = first // P + 2 * c + half
                o = gated[:, T * half:T * half + T] if dst is None else dst[:, 2 * c + half, :]
                m2 = TS(o, pad[:, half, 0:T], vec("conv_d", blk), ALU.mult, marks=[m])
                for k in range(1, 3):
                    m2 = STT(o, pad[:, half, k:k + T], vec("conv_d", k * 3 * JB + blk), o, ALU.mult, ALU.add, marks=[m2])
                if dst is None:
                    m2 = VV(PROD[:, 2 * c + half, :], PROD[:, 2 * c + half, :], o, ALU.mult, marks=[m2])
        return m2

    fill(pad, 0.0, act.last())
    m_pad = dve.last()
    act.after(m_pad)
    catch_up()
    short_conv(0)
    catch_up(True)
    m_roped = roped[-1]

    def scores(h, e_free):
        E, stat = exps[h % 2], head_stats[:, h % 2, :].rearrange("p (b s) -> p b s", b=4)
        pe.after(m_roped)
        got, exp = [], []
        for b in range(4):
            pe.after(bank_read[b])
            got.append(pe.done(mm(banks[b][:, :], Q[64 * (b % 2):64 * (b % 2) + 64, h, P * (b // 2):P * (b // 2) + P],
                                  K[64 * (b % 2):64 * (b % 2) + 64, h, :], True, True)))
        for b in range(4):
            m = RED(stat[:, b, 0:1], banks[b][:, :], ALU.max, marks=[got[b], e_free], negate=True)
            m = bank_read[b] = A(E[:, b, :], banks[b][:, :], ACT.Exp, m, bias=stat[:, b, 0:1], accum=stat[:, b, 1:2])
            exp.append(m)
        for qt in range(TT):
            b0, b1 = 2 * qt, 2 * qt + 1
            m = RECIP(stat[:, b0:b0 + 2, 2:3], stat[:, b0:b0 + 2, 1:2], exp[b0], exp[b1])
            m = VV(stat[:, b1, 3:4], stat[:, b1, 2:3], lam[:, 0:1], ALU.mult, marks=[m, m_lam])
            m = TS(E[:, b1, :], E[:, b1, :], stat[:, b1, 3:4], ALU.mult, marks=[m])
            m = STT(E[:, b0, :], E[:, b0, :], stat[:, b0, 2:3], E[:, b1, :], ALU.mult, ALU.subtract, marks=[m])
        return m

    def values(h, m):
        E = exps[h % 2]
        for qt in range(TT):
            pe.after(bank_read[4])
            for kb in range(4):
                ins = turn_over(banks[4][:, P * kb:P * kb + P], E[:, 2 * qt, P * kb:P * kb + P], m)
            turned = pe.done(ins)
            m_t = bank_read[4] = copy_a(PT[:, :, P * qt:P * qt + P], banks[4][:, :].rearrange("p (k q) -> p k q", k=4),
                                        turned, m_roped)
        pe.after(bank_read[5])
        pe.after(m_t, m_vcopy)
        for kb in range(4):
            ins = mm(banks[5][:, 0:T], V[:, kb, P * h:P * h + P], PT[:, kb, :], kb == 0, kb == 3)
        got = pe.done(ins)
        m = A(Y[:, h, :], banks[5][:, 0:T], ACT.Square, got)
        pe.after(m)
        m = pe.done(mm(banks[5][:, T:2 * T], ones, Y[:, h, :], True, True))
        _, m = inverse_rms(Y[:, h, :], banks[5][:, T:2 * T], 1.0 / P, SUB, m)
        bank_read[5] = STT(Y[:, h, :], banks[5][:, 0:T], gsub, Y[:, h, :], ALU.mult, ALU.mult, marks=[m, m_gsub])
        return turned

    def spectrum(m):
        for t in range(TT):
            b = 6 + t
            pe.after(bank_read[b])
            for blk in range(JB):
                ins = turn_over(banks[b][:, P * blk:P * blk + P], PROD[:, blk, P * t:P * t + P], m)
            m2 = bank_read[b] = copy_a(UT[:, t, :], banks[b][:, :], pe.done(ins))
        pe.after(m2)
        for f in range(4):
            b = 6 + f % 2
            pe.after(bank_read[b])
            for t in range(TT):
                ins = mm(banks[b][:, :], dft[:, t, P * f:P * f + P], UT[:, t, :], t == 0, t == TT - 1)
            m = bank_read[b] = copy_v(UF[:, f, :], banks[b][:, :], pe.done(ins))
        for f in range(2):
            re, im, hre, him = UF[:, f, :], UF[:, 2 + f, :], HF[:, f, :], HF[:, 2 + f, :]
            m1 = VV(t1, re, hre, ALU.mult, marks=[m])
            m2 = VV(t2, im, him, ALU.mult)
            m3 = VV(him, re, him, ALU.mult, marks=[m2])
            m4 = VV(hre, im, hre, ALU.mult, marks=[m1])
            VV(re, t1, t2, ALU.subtract, marks=[m4])
            m = VV(im, him, hre, ALU.add, marks=[m4])
        return m

    def back_in_time(m):
        pe.after(m, m_middle)
        for blk in range(JB):
            b = 6 + blk % 2
            pe.after(bank_read[b])
            for f in range(4):
                ins = mm(banks[b][:, 0:T], UF[:, f, P * blk:P * blk + P], idft[:, f, :], f == 0, f == 3)
            m = bank_read[b] = STT(Y[:, HEADS + blk, :], PROD[:, blk, :], vec("hf_bias", blk), banks[b][:, 0:T],
                                   ALU.mult, ALU.add, marks=[pe.done(ins)])
            m = VV(Y[:, HEADS + blk, :], Y[:, HEADS + blk, :], GO[:, blk, :], ALU.mult, marks=[m])
        return m

    p0 = scores(0, pe.last())
    m_prod = short_conv(1)
    p1 = scores(1, pe.last())
    e0 = values(0, p0)
    p2 = scores(2, e0)
    m_freq = spectrum(m_prod)
    e1 = values(1, p1)
    p3 = scores(3, e1)
    values(2, p2)
    m_hy = back_in_time(m_freq)
    attention_done = [q.last() for q in (pe, act, dve)]
    values(3, p3)
    carve = Carve()
    NA_BIAS = carve(NA_H, TT, T)
    GATES = carve(2 * KB, T)
    HID = carve(FB, T)
    assert BLOCK1_END <= carve.at
    NA_MASK = carve(TT, T)
    SW_BIAS = carve(SW_H, TT, T)
    by_the_way = Carve(0, KB * T, ctx_u)
    sw_mask, hot, table, dist = by_the_way(TT, T), by_the_way(2 * T), by_the_way(SW_H), by_the_way(2 * T)
    in_late, out_dist, in_bias = counted("in_late"), counted("out_distance"), counted("in_sw_bias")
    pool.after(attention_done)
    late = [load(in_late, NA_MASK.rearrange("p t k -> p (t k)"), a["late"][:, 0:512], pool),
            load(in_late, sw_mask.rearrange("p t k -> p (t k)"), a["late"][:, 512:1024], pool),
            load(in_late, hot, a["late"][:, 1024:1536], pool),
            load(in_late, table[0:32, :], a["t5_rel_table_2"], pool)][-1]
    project_back(a["w_out_cd"][0], Y, 1, (0,), [m_hy, dve.last()])
    pe.after(bank_read[0])
    pe.after(late)
    m = pe.done(mm(banks[0][0:SW_H, :], table[0:32, :], hot[0:32, :], True, True))
    m = bank_read[0] = copy_a(dist[0:SW_H, :], banks[0][0:SW_H, :], m)
    scratch = nc.dram_tensor("distance_bias", (SW_H, 2 * T), F32, kind="Internal").ap()
    m = load(out_dist, scratch, dist[0:SW_H, :], pool, [m])
    for t in range(TT):
        pairs = bass.AP(tensor=scratch.tensor, offset=P - P * t, ap=[[1, P], [2 * T, SW_H], [1, T]])
        m_pairs = load(in_bias, SW_BIAS[:, :, t, :], pairs, pool, [m])
    for t in range(TT):
        pool.after(m_pairs)
        m_sw_bias = pool.done(nc.gpsimd.tensor_tensor(
            SW_BIAS[:, :, t, :], SW_BIAS[:, :, t, :],
            sw_mask[:, t, :].rearrange("p (o k) -> p o k", o=1).broadcast_to([P, SW_H, T]), ALU.add))

    moe(1, (0,), sq)

    meet()
    h0 = H[:, 0]
    spare = H[:, 1].rearrange("p k t -> p (k t)")
    OUT2 = U[:, 1]
    merged = H[:, 1]
    free_g = Carve(0, 2 * KB * T, GATES.rearrange("p n t -> p (n t)"))
    var, rinv = free_g(13, T), free_g(T)
    sg = [GATES.rearrange("p n t -> p (n t)")[:, 512 * n:512 * n + 512] for n in range(2)]
    heads = Carve(0, FB * T, HID.rearrange("p n t -> p (n t)"))
    QA, KA, QS, KS, KSX = heads(4, T), heads(4, T), heads(4, T), heads(T), heads(T)
    VA, VS = heads(TT, 512), heads(TT, P)
    sq = spare[:, 0:1024]
    SC = [spare[:, 512 * n:512 * n + 512].rearrange("p (t k) -> p t k", t=TT) for n in range(2)]
    PT = [spare[:, 1024 + 512 * n:1536 + 512 * n].rearrange("p (k q) -> p k q", k=TT) for n in range(2)]
    g8 = small[:, 0:2]
    stats = small[:, 16:16 + 16 * 8]
    in_bias_na = counted("in_na_bias")

    def now(name, i=0):
        c = LVEC[name][0] + i
        return cur[:, c:c + 1]

    def load_na_bias(l):
        for r in range(ROWS):
            for kr in range(ROWS):
                src = bass.AP(tensor=a["na_rpb_2"].tensor, ap=[[1, GRID], [RPB_R * RPB_C, NA_H], [1, GRID]],
                              offset=l * (NA_H * RPB_R * RPB_C) + (kr - r + 7) * RPB_C + 15 - (GRID - 1))
                p0 = GRID * (1 - r % 2)
                m = load(in_bias_na, NA_BIAS[p0:p0 + GRID, :, r // 2, GRID * kr:GRID * kr + GRID], src)
        return m

    def reversed_queries(x):
        return x.rearrange("p (n q) -> p n q", q=P)[:, :, ::-1]

    with turns_of(nc, "layers", LAYERS, [*workers, sp],
                  [*(q.count for q in workers), chunks_read, *landed, in_bias_na], known, made) as (loop, l):
        meet()
        first = issued[0]
        read = {b: None for b in range(8)}

        def chunk(w, rows, cols):
            tile, there = fetch(w[l, rows, cols])
            pe.after(there)
            return tile

        def wide(w, c):
            return chunk(w, slice(0, D), slice(256 * c, 256 * c + 256))

        h_ready = [None] * KB
        m = copy_v(cur[:, :], lvec_mem[:, bass.ds(l * NLVEC, NLVEC)], m_layers)
        m_sink = copy_v(small[:, 2:2 + SW_H], sink_mem[:, bass.ds(l * SW_H, SW_H)])
        m = TS(g8[:, 0:1], now("na_q_norm"), DH ** -0.5, ALU.mult, marks=[m])
        m_g8 = TS(g8[:, 1:2], now("sw_q_norm"), DH ** -0.5, ALU.mult)
        def sums(b, sq):
            bank_read[b] = read[b]
            return b, sum_squares(b, (0,), sq, h_ready)

        def normed(name, sums_at):
            b, m_sum = sums_at
            m = inverse_root(b, T, rinv, m_sum)
            read[b] = bank_read[b]
            return [STT(U[:, 0, k, :], h0[:, k, :], now(name, k), rinv, ALU.mult, ALU.mult, marks=[m])
                    for k in range(KB)]

        def project(tile, b, ready, halves_=2):
            pe.after(read[b])
            for half in range(halves_):
                for k in range(KB):
                    pe.after(ready[k])
                    ins = mm(banks[b][:, T * half:T * half + T], tile[:, k, P * half:P * half + P], U[:, 0, k, :],
                             k == 0, k == KB - 1)
            return (chunks_read if halves_ == 2 else pe.count).step(ins)

        def ffn(n, sums_at, idle=0, beside=lambda: None):
            gate, up, down = (a[f"ffn{n}_w_{x}_2"] for x in ("gate", "up", "down"))
            ready = normed(f"ffn{n}_norm", sums_at)
            returned = beside()
            for c in range(FB // 2):
                b = c % 2
                m = project(wide(gate, c), b, ready)
                m_s = read[b] = A(sg[c % 2], banks[b][:, :], ACT.Silu, m, dve.last())
                m = project(wide(up, c), 2 + b, ready)
                m_h = read[2 + b] = VV(HID[:, 2 * c:2 * c + 2, :].rearrange("p n t -> p (n t)"), banks[2 + b][:, :],
                                       sg[c % 2], ALU.mult, marks=[m, m_s])
            pe.after(*(read[b] for b in range(4, 8)))
            for c in range(FB // 2):
                w = chunk(down, slice(256 * c, 256 * c + 256), slice(0, D))
                pe.after(m_h)
                for kk in range(2):
                    k = 2 * c + kk
                    for n in range(KB):
                        ins = mm(banks[4 + n // 2][:, T * (n % 2):T * (n % 2) + T], w[:, kk, P * n:P * n + P],
                                 HID[:, k, :], k == 0 and n % 2 == 0, k == FB - 1)
                m = chunks_read.step(ins, 1 + (idle if c == FB // 2 - 1 else 0))
            for p in range(KB // 2):
                h_ready[2 * p] = h_ready[2 * p + 1] = read[4 + p] = STT(h0[:, 2 * p:2 * p + 2, :], banks[4 + p][:, :].rearrange("p (n t) -> p n t", n=2), 0.5,
                                  h0[:, 2 * p:2 * p + 2, :], ALU.mult, ALU.add, marks=[m])
            return returned

        def na_bias():
            m_rpb = load_na_bias(l)
            for t in range(TT):
                pool.after(m_rpb, late)
                m = pool.done(nc.gpsimd.tensor_tensor(
                    NA_BIAS[:, :, t, :], NA_BIAS[:, :, t, :],
                    NA_MASK[:, t, :].rearrange("p (o k) -> p o k", o=1).broadcast_to([P, NA_H, T]), ALU.add))
            return m

        m_na_bias = ffn(1, sums(7, sq), beside=na_bias)
        sums_at = sums(0, sq)
        meet()

        ready = normed("mix_norm", sums_at)
        n_var, later, m_v2 = 0, None, None

        def head_norms(b, n, v, m, slot, dst, gain, queries=False):
            w = T * n
            to, got = sq[:, 512 * slot:512 * slot + w], banks[b][:, 0:w]
            if queries:
                to, got = reversed_queries(to), got.rearrange("p (n q) -> p n q", q=P)
            m = read[b] = A(to, got, ACT.Square, m, pe.last())
            pe.after(m, read[6])
            m = pe.done(mm(banks[6][:, 0:w], halves, sq[:, 512 * slot:512 * slot + w], True, True))
            inv = var[:, v:v + n, :].rearrange("p n t -> p (n t)")
            read[6], m = inverse_rms(inv, banks[6][:, 0:w], 1.0 / DH, MAIN, m)
            return STT(dst, dst, gain, inv, ALU.mult, ALU.mult, marks=[m, m_g8])

        flip = [0]

        def next_bank():
            flip[0] ^= 1
            return 4 + flip[0]

        w_in = a["w_in_2"]

        def heads_in(dst, v, first_chunk, gain, queries=False):
            nonlocal later
            for c in range(2):
                b = next_bank()
                m = project(wide(w_in, first_chunk + c), b, ready)
                if later:
                    later()
                to, got = dst[:, 2 * c:2 * c + 2, :].rearrange("p n t -> p (n t)"), banks[b][:, :]
                if queries:
                    to, got = reversed_queries(to), got.rearrange("p (n q) -> p n q", q=P)
                m = read[b] = copy_v(to, got, m)
                part = dst[:, 2 * c:2 * c + 2, :].rearrange("p n t -> p (n t)")
                later = lambda b=b, c=c, m=m, part=part: head_norms(b, 2, v + 2 * c, m, flip[0], part, gain, queries)

        heads_in(QA, 0, 0, g8[:, 0:1], True)
        heads_in(KA, 4, 2, now("na_k_norm"))
        heads_in(QS, 8, 6, g8[:, 1:2], True)
        tile = wide(w_in, 8)
        b = next_bank()
        m = project(tile, b, ready, 1)
        later()
        m = copy_v(KS, banks[b][:, 0:T], m)
        later = lambda b=b, m=m, slot=flip[0]: head_norms(b, 1, 12, m, slot, KS, now("sw_k_norm"))
        b = 3
        pe.after(read[b])
        for t in range(TT):
            for k in range(KB):
                ins = mm(banks[b][:, P * t:P * t + P], U[:, 0, k, P * t:P * t + P], tile[:, k, P:2 * P], k == 0, k == KB - 1)
        m = chunks_read.step(ins)
        m_vs = read[b] = copy_v(VS.rearrange("p t n -> p (t n)"), banks[b][:, 0:T], m)
        tiles = [wide(w_in, 4), wide(w_in, 5)]
        for t in range(TT):
            b = next_bank()
            pe.after(read[b])
            for c in range(2):
                for k in range(KB):
                    ins = mm(banks[b][:, 256 * c:256 * c + 256], U[:, 0, k, P * t:P * t + P], tiles[c][:, k, :],
                             k == 0, k == KB - 1)
            m = chunks_read.step(ins, 2) if t == TT - 1 else pe.done(ins)
            if t == 0:
                m_ks = later()
            m_va = read[b] = copy_v(VA[:, t, :], banks[b][:, :], m)

        gate_tile = [None]

        def gates(n):
            c, half = divmod(n, 2)
            if half == 0:
                gate_tile[0] = wide(w_in, 9 + c)
            b = next_bank()
            pe.after(read[b])
            for k in range(KB):
                ins = mm(banks[b][:, 0:T], gate_tile[0][:, k, P * half:P * half + P], U[:, 0, k, :], k == 0, k == KB - 1)
            m = (chunks_read if half else pe.count).step(ins)
            read[b] = A(GATES[:, n, :], banks[b][:, 0:T], ACT.Sigmoid, m, m_normed, bias=now("b_gate", n))

        m_normed = copy_v(KSX[0:DH, :], KS[DH:P, :], m_ks)
        m_normed = copy_v(KSX[DH:P, :], KS[0:DH, :], m_ks)

        NA, SW = 0, 1
        work = [(kind, h) for kind in (NA, SW) for h in range(NA_H)]
        probs_read = [None, None]

        def scores(n):
            kind, h = work[n]
            p0, blk, b, i = DH * (h % 2), h // 2, n % 2, n % 2
            q = (QS if kind else QA)[p0:p0 + DH, blk, :]
            if kind:
                k = (KS if (h // 4) == h % 2 else KSX)[p0:p0 + DH, :]
            else:
                k = KA[p0:p0 + DH, blk, :]
            pe.after(read[b], m_normed)
            for t in range(TT):
                ins = mm(banks[b][:, T * t:T * t + T], q[:, P * t:P * t + P], k, True, True)
            m = pe.done(ins)
            bias = (SW_BIAS if kind else NA_BIAS)[:, h]
            m = read[b] = VV(SC[i], banks[b][:, :].rearrange("p (t k) -> p t k", t=TT), bias, ALU.add,
                             marks=[m, m_na_bias, m_sw_bias, probs_read[i]])
            st = stats[:, 64 * i:64 * i + 64]
            top, total, extra = st[:, 0:2], st[:, 2:4], st[:, 4:6]
            m = RED(top, SC[i], ALU.max, marks=[m], negate=True)
            if kind:
                m = TS(top, top, -1.0, ALU.mult, small[:, 2 + h:3 + h], ALU.max, marks=[m, m_sink])
                m = TS(top, top, -1.0, ALU.mult, marks=[m])
                A(extra, top, ACT.Exp, m, bias=small[:, 2 + h:3 + h])
            for t in range(TT):
                m_e = A(SC[i][:, t, :], SC[i][:, t, :], ACT.Exp, m, bias=top[:, t:t + 1], accum=total[:, t:t + 1])
            if kind:
                m_e = VV(total, total, extra, ALU.add, marks=[m_e])
            m = RECIP(total, total, m_e)
            for t in range(TT):
                m2 = TS(SC[i][:, t, :], SC[i][:, t, :], total[:, t:t + 1], ALU.mult, marks=[m])
            return m2

        def turn(n, m):
            i = n % 2
            pe.after(read[2], m)
            for k in range(TT):
                for t in range(TT):
                    ins = turn_over(banks[2][:, T * k + P * t:T * k + P * t + P], SC[i][:, t, P * k:P * k + P])
            probs_read[i] = pe.done(ins)
            m = read[2] = copy_a(reversed_queries(PT[i].rearrange("p k q -> p (k q)")),
                                 banks[2][:, :].rearrange("p (n q) -> p n q", q=P), probs_read[i], turned_read[i])
            return m

        def values(n, m):
            kind, h = work[n]
            p0, blk, i = DH * (h % 2), h // 2, n % 2
            pe.after(m, read[3], m_va, m_vs)
            for k in range(TT):
                v = VS[:, k, DH * (h // 4):DH * (h // 4) + DH] if kind else VA[:, k, DH * h:DH * h + DH]
                ins = mm(banks[3][p0:p0 + DH, 0:T], v, PT[i][:, k, :], k == 0, k == TT - 1)
            m = turned_read[i] = pe.done(ins)
            if h % 2:
                read[3] = copy_a(OUT2[:, 4 * kind + blk, :], banks[3][:, 0:T], m)

        turned_read, m_probs, m_turned = [None, None], [], []
        for n in range(len(work) + 2):
            if n < len(work):
                m_probs.append(scores(n))
            if n > 1:
                values(n - 2, m_turned[n - 2])
            if n < len(work):
                gates(n)
            if 0 < n <= len(work):
                m_turned.append(turn(n - 1, m_probs[n - 1]))
        m_attn = act.last()

        tiles = [chunk(w, slice(0, 512), slice(512 * c, 512 * c + 512))
                 for w in (a["w_branch_na_2"], a["w_branch_sw_2"]) for c in range(2)]
        pe.after(m_attn)
        t1 = [KA[:, 0:2, :].rearrange("p n t -> p (n t)"), KA[:, 2:4, :].rearrange("p n t -> p (n t)")]
        merged_at = []
        for p in range(KB // 2):
            c, off = divmod(p, 2)
            got = []
            for branch in range(2):
                b = 2 * (p % 2) + branch
                pe.after(read[b])
                for half in range(2):
                    for k in range(4):
                        ins = mm(banks[b][:, T * half:T * half + T],
                                 tiles[2 * branch + c][:, k, 256 * off + P * half:256 * off + P * half + P],
                                 OUT2[:, 4 * branch + k, :], k == 0, k == 3)
                got.append(chunks_read.step(ins, 4) if (p, branch) == (KB // 2 - 1, 1) else pe.done(ins))
            for branch in range(2):
                b = 2 * (p % 2) + branch
                g = GATES[:, KB * branch + 2 * p:KB * branch + 2 * p + 2, :].rearrange("p n t -> p (n t)")
                m = read[b] = VV(t1[branch], banks[b][:, :], g, ALU.mult, marks=[got[branch], m_attn, dve.last()])
            m = VV(merged[:, 2 * p:2 * p + 2, :].rearrange("p n t -> p (n t)"), t1[0], t1[1], ALU.add, marks=[m])
        pe.after(m)
        for c in range(KB // 2):
            tile, b = wide(a["w_out_2"], c), c % 4
            pe.after(read[b])
            for half in range(2):
                for k in range(KB):
                    ins = mm(banks[b][:, T * half:T * half + T], tile[:, k, P * half:P * half + P], merged[:, k, :],
                             k == 0, k == KB - 1)
            m = chunks_read.step(ins)
            h_ready[2 * c] = h_ready[2 * c + 1] = read[b] = VV(
                         h0[:, 2 * c:2 * c + 2, :].rearrange("p n t -> p (n t)"),
                         h0[:, 2 * c:2 * c + 2, :].rearrange("p n t -> p (n t)"), banks[b][:, :], ALU.add, marks=[m])
        sums_at = sums(6, QA.rearrange("p n t -> p (n t)"))
        meet()
        idle = -(issued[0] + 3 * FB // 2 - first) % SLOTS
        ffn(2, sums_at, idle)
        issued[0] += idle
    issued[0] = chunks_read.n

    sent = counted("sent")
    sp.after([q.last() for q in workers], m_layers)
    sent.step(nc.sync.dma_start(out.rearrange("(k p) t -> p k t", p=P), h0))
    sp.after(Mark(sent, sent.n))
    return made


_WEIGHTS = ["w_ada", "w_in_ab", "w_out_ab", "w_in_cd", "w_out_cd", "w_gate", "w_up", "w_down", "hf_w1", "hf_w2",
            "hf_w3", "sw_sink_2", "t5_rel_table_2", "na_rpb_2", "ffn1_w_gate_2", "ffn1_w_up_2", "ffn1_w_down_2",
            "w_in_2", "w_branch_na_2", "w_branch_sw_2", "w_out_2", "ffn2_w_gate_2", "ffn2_w_up_2", "ffn2_w_down_2"]


def lay_out(inputs):
    given = {n: np.asarray(v) for n, v in inputs.items()}
    out = {n: np.ascontiguousarray(given[n]) for n in _WEIGHTS}
    out["x_t"] = np.ascontiguousarray(given["x"][0].T)
    out["ctx_t"] = np.ascontiguousarray(given["ctx"][0].T)
    out["vectors"] = pack_vectors(given)
    out["layer_vectors"] = pack_layer_vectors(given)
    out["kept"], out["early"], out["middle"], out["late"] = (kept_constants(), early_constants(), middle_constants(),
                                                            late_constants())
    return out


def kernel(**inputs):
    from concourse import bacc
    from concourse.bass_utils import run_bass_kernel_spmd

    arrays = lay_out(inputs)

    def build(known):
        nc = bacc.Bacc("TRN2", target_bir_lowering=False, num_devices=1)
        args = {n: nc.dram_tensor(f"in_{n}", v.shape, mybir.dt.from_np(v.dtype), kind="ExternalInput").ap()
                for n, v in arrays.items()}
        out = nc.dram_tensor("out", (D, T), F32, kind="ExternalOutput").ap()
        return nc, program(nc, args, out, known)

    _, known = build({})
    nc, _ = build(known)
    r = run_bass_kernel_spmd(nc, [{f"in_{n}": v for n, v in arrays.items()}], core_ids=[0])
    return np.ascontiguousarray(r.results[0]["out"].T)[None]
```
